# Optimizing a Trainium2 kernel written in Bass

```python
import jax, jax.numpy as jnp
from jax import lax
import numpy as np

D_MODEL = 1024
BATCH = 1
SEQ = 256
DEPTH = 1

CTX_LEN = 256
GRID_W = 64
D_RNN = 1024
RNN_HEADS = 4
RNN_HEAD_DIM = D_RNN // RNN_HEADS
CONV_W = 4
LRU_C = 8.0
D_POOL = 1024
POOL_WINDOWS = (2, 4, 8, 16)
POOL_GROUP = D_POOL // len(POOL_WINDOWS)
IN_COLS = 2 * D_RNN + D_POOL + 2 * D_MODEL
N_EXPERTS = 32
TOP_K = 4
D_FF = 1024
SWIGLU_LIMIT = 7.0
SWIGLU_ALPHA = 1.702
EPS = 1e-6

kernel_name = 'hybrid_rglru_pool_moe_block'

def rmsnorm(x, g):
    xf = x.astype(jnp.float32)
    y = xf * lax.rsqrt(jnp.mean(xf * xf, axis=-1, keepdims=True) + EPS)
    return (y * g.astype(jnp.float32)).astype(x.dtype)

def modulate(u, shift, scale):
    return u * (1 + scale) + shift

def dwconv_centred(x, w, b):
    left = CONV_W // 2
    y = lax.conv_general_dilated(x, w[:, None, :], window_strides=(1,),
                                 padding=[(left, CONV_W - 1 - left)],
                                 dimension_numbers=('NWC', 'WIO', 'NWC'),
                                 feature_group_count=x.shape[-1])
    return y + b

def lru_coeffs(xc, wa, ba, wx, bx, lam):
    bsz, t = xc.shape[:2]
    xh = xc.reshape(bsz, t, RNN_HEADS, RNN_HEAD_DIM)
    r = jax.nn.sigmoid(jnp.einsum('bthi,hij->bthj', xh, wa).reshape(bsz, t, D_RNN) + ba)
    i = jax.nn.sigmoid(jnp.einsum('bthi,hij->bthj', xh, wx).reshape(bsz, t, D_RNN) + bx)
    log_a = -LRU_C * r.astype(jnp.float32) * jax.nn.softplus(-lam.astype(jnp.float32))
    a = jnp.exp(log_a)
    mult = jnp.sqrt(-jnp.expm1(2.0 * log_a))
    b = mult * (i * xc).astype(jnp.float32)
    return a, b

def _combine(left, right):
    a_l, b_l = left
    a_r, b_r = right
    return a_l * a_r, a_r * b_l + b_r

def linear_scan(a, b, h0):
    if h0 is not None:
        b = b.at[:, 0].add(a[:, 0] * h0)
    _, h = lax.associative_scan(_combine, (a, b), axis=1)
    return h

def recurrent_states(x_rnn, conv_w, conv_b, wa, ba, wx, bx, lam, h0_f, h0_b):
    xc = dwconv_centred(x_rnn, conv_w, conv_b)
    a_f, b_f = lru_coeffs(xc, wa[0], ba[0], wx[0], bx[0], lam[0])
    a_b, b_b = lru_coeffs(xc, wa[1], ba[1], wx[1], bx[1], lam[1])
    h_f = linear_scan(a_f, b_f, h0_f)
    h_b = jnp.flip(linear_scan(jnp.flip(a_b, 1), jnp.flip(b_b, 1), h0_b), 1)
    return h_f, h_b

def pool_mixer(xp, n_rows, w_grp, scale):
    bsz, t, _ = xp.shape
    line = t // n_rows
    xf = xp.reshape(bsz, n_rows, line, D_POOL).astype(jnp.float32)
    cs = jnp.pad(jnp.cumsum(xf, axis=2), ((0, 0), (0, 0), (1, 0), (0, 0)))
    pos = jnp.arange(line)
    diffs = []
    for gi, w in enumerate(POOL_WINDOWS):
        lo = jnp.clip(pos - w // 2, 0, line)
        hi = jnp.clip(pos + w - w // 2, 0, line)
        seg = cs[..., gi * POOL_GROUP:(gi + 1) * POOL_GROUP]
        mean = (jnp.take(seg, hi, axis=2) - jnp.take(seg, lo, axis=2)) / (hi - lo).astype(jnp.float32)[:, None]
        diffs.append(mean - xf[..., gi * POOL_GROUP:(gi + 1) * POOL_GROUP])
    d = jnp.stack(diffs, axis=-2).astype(xp.dtype)
    y = jnp.einsum('brlgi,gij->brlgj', d, w_grp)
    return y.reshape(bsz, t, D_POOL) * scale

def mixer(u, n_rows, h0_f, h0_b, w_in, conv_w, conv_b, wa, ba, wx, bx, lam,
          pool_w, pool_scale, w_rnn_proj, w_pool_proj, w_out):
    proj = u @ w_in
    x_rnn, g_rnn, x_pool, m_rnn, m_pool = jnp.split(
        proj, [D_RNN, 2 * D_RNN, 2 * D_RNN + D_POOL, 2 * D_RNN + D_POOL + D_MODEL], axis=-1)
    h_f, h_b = recurrent_states(x_rnn, conv_w, conv_b, wa, ba, wx, bx, lam, h0_f, h0_b)
    y_rnn = (h_f + h_b).astype(u.dtype) * jax.nn.gelu(g_rnn)
    y_pool = pool_mixer(x_pool, n_rows, pool_w, pool_scale)
    merged = jax.nn.sigmoid(m_rnn) * (y_rnn @ w_rnn_proj) + jax.nn.sigmoid(m_pool) * (y_pool @ w_pool_proj)
    return merged @ w_out, h_f, h_b

def moe(h, w_r, b_r, w1, b1, w2, b2):
    logits = (h @ w_r + b_r).astype(jnp.float32)
    top_v, top_i = lax.top_k(logits, TOP_K)
    top_w = jax.nn.softmax(top_v, axis=-1)
    comb = jnp.einsum('nk,nke->ne', top_w, jax.nn.one_hot(top_i, N_EXPERTS, dtype=jnp.float32)).astype(h.dtype)
    out = jnp.zeros_like(h)
    for e in range(N_EXPERTS):
        z = h @ w1[e] + b1[e]
        glu = jnp.minimum(z[:, :D_FF], SWIGLU_LIMIT)
        lin = jnp.clip(z[:, D_FF:], -SWIGLU_LIMIT, SWIGLU_LIMIT)
        act = glu * jax.nn.sigmoid(SWIGLU_ALPHA * glu) * (lin + 1)
        out = out + comb[:, e:e + 1] * (act @ w2[e] + b2[e])
    return out

def setup_inputs(seed: int = 0) -> dict:
    key = jax.random.key(seed)
    ks = iter(jax.random.split(key, 40))
    f32 = jnp.float32
    L = DEPTH

    def nrm(shape, scale):
        return jax.random.normal(next(ks), shape, f32) * scale

    def gain(shape):
        return 1.0 + 0.05 * jax.random.normal(next(ks), shape, f32)

    u = jax.random.uniform(next(ks), (L, 2, D_RNN), f32, minval=0.9, maxval=0.999)
    a0 = u ** (1.0 / LRU_C)
    lam = jnp.log(a0) - jnp.log1p(-a0)
    return {
        'x': nrm((BATCH, SEQ, D_MODEL), 1.0),
        'c': nrm((BATCH, D_MODEL), 1.0),
        'ctx': nrm((BATCH, CTX_LEN, D_MODEL), 1.0),
        'c_ctx': nrm((D_MODEL,), 1.0),
        'w_mod': nrm((L, D_MODEL, 6 * D_MODEL), 0.5 * D_MODEL ** -0.5),
        'b_mod': nrm((L, 6 * D_MODEL), 0.02),
        'norm_pre_mix': gain((L, D_MODEL)),
        'norm_post_mix': gain((L, D_MODEL)),
        'norm_pre_ffn': gain((L, D_MODEL)),
        'norm_post_ffn': gain((L, D_MODEL)),
        'w_in': nrm((L, D_MODEL, IN_COLS), D_MODEL ** -0.5),
        'conv_w': nrm((L, CONV_W, D_RNN), CONV_W ** -0.5),
        'conv_b': nrm((L, D_RNN), 0.02),
        'lru_wa': nrm((L, 2, RNN_HEADS, RNN_HEAD_DIM, RNN_HEAD_DIM), RNN_HEAD_DIM ** -0.5),
        'lru_ba': nrm((L, 2, D_RNN), 0.02),
        'lru_wx': nrm((L, 2, RNN_HEADS, RNN_HEAD_DIM, RNN_HEAD_DIM), RNN_HEAD_DIM ** -0.5),
        'lru_bx': nrm((L, 2, D_RNN), 0.02),
        'lru_lambda': lam,
        'pool_w': nrm((L, len(POOL_WINDOWS), POOL_GROUP, POOL_GROUP), POOL_GROUP ** -0.5),
        'pool_scale': 1.0 + 0.1 * jax.random.normal(next(ks), (L, D_POOL), f32),
        'w_rnn_proj': nrm((L, D_RNN, D_MODEL), D_RNN ** -0.5),
        'w_pool_proj': nrm((L, D_POOL, D_MODEL), D_POOL ** -0.5),
        'w_out': nrm((L, D_MODEL, D_MODEL), D_MODEL ** -0.5),
        'router_w': nrm((L, D_MODEL, N_EXPERTS), D_MODEL ** -0.5),
        'router_b': nrm((L, N_EXPERTS), 0.01),
        'exp_w1': nrm((L, N_EXPERTS, D_MODEL, 2 * D_FF), D_MODEL ** -0.5),
        'exp_b1': nrm((L, N_EXPERTS, 2 * D_FF), 0.02),
        'exp_w2': nrm((L, N_EXPERTS, D_FF, D_MODEL), D_FF ** -0.5),
        'exp_b2': nrm((L, N_EXPERTS, D_MODEL), 0.02),
    }

def reference(x, c, ctx, c_ctx, w_mod, b_mod, norm_pre_mix, norm_post_mix, norm_pre_ffn,
              norm_post_ffn, w_in, conv_w, conv_b, lru_wa, lru_ba, lru_wx, lru_bx, lru_lambda,
              pool_w, pool_scale, w_rnn_proj, w_pool_proj, w_out, router_w, router_b,
              exp_w1, exp_b1, exp_w2, exp_b2):
    bsz, seq, d = x.shape
    rows = seq // GRID_W
    for l in range(DEPTH):
        last = l == DEPTH - 1
        mod_lat = (jax.nn.silu(c) @ w_mod[l] + b_mod[l])[:, None, :]
        mod_ctx = jax.nn.silu(c_ctx) @ w_mod[l] + b_mod[l]
        sh1, sc1, g1, sh2, sc2, g2 = jnp.split(mod_lat, 6, axis=-1)
        csh1, csc1, cg1, csh2, csc2, cg2 = jnp.split(mod_ctx, 6, axis=-1)
        mix_w = (w_in[l], conv_w[l], conv_b[l], lru_wa[l], lru_ba[l], lru_wx[l], lru_bx[l],
                 lru_lambda[l], pool_w[l], pool_scale[l], w_rnn_proj[l], w_pool_proj[l], w_out[l])

        u_ctx = modulate(rmsnorm(ctx, norm_pre_mix[l]), csh1, csc1)
        if last:
            hc_f, hc_b = recurrent_states(u_ctx @ w_in[l][:, :D_RNN], conv_w[l], conv_b[l],
                                          lru_wa[l], lru_ba[l], lru_wx[l], lru_bx[l],
                                          lru_lambda[l], None, None)
        else:
            m_ctx, hc_f, hc_b = mixer(u_ctx, 1, None, None, *mix_w)

        u_lat = modulate(rmsnorm(x, norm_pre_mix[l]), sh1, sc1)
        m_lat, _, _ = mixer(u_lat, rows, hc_f[:, -1], hc_b[:, 0], *mix_w)
        x = x + g1 * rmsnorm(m_lat, norm_post_mix[l])
        if not last:
            ctx = ctx + cg1 * rmsnorm(m_ctx, norm_post_mix[l])

        moe_w = (router_w[l], router_b[l], exp_w1[l], exp_b1[l], exp_w2[l], exp_b2[l])
        v_lat = modulate(rmsnorm(x, norm_pre_ffn[l]), sh2, sc2).reshape(-1, d)
        if last:
            f_lat = moe(v_lat, *moe_w).reshape(bsz, seq, d)
        else:
            v_ctx = modulate(rmsnorm(ctx, norm_pre_ffn[l]), csh2, csc2).reshape(-1, d)
            f_all = moe(jnp.concatenate([v_lat, v_ctx], axis=0), *moe_w)
            f_lat = f_all[:bsz * seq].reshape(bsz, seq, d)
            f_ctx = f_all[bsz * seq:].reshape(ctx.shape)
            ctx = ctx + cg2 * rmsnorm(f_ctx, norm_post_ffn[l])
        x = x + g2 * rmsnorm(f_lat, norm_post_ffn[l])
    return x


_drawn_inputs = setup_inputs


def setup_inputs(seed=0):
    import zlib

    import numpy as np

    out = dict(_drawn_inputs(seed))
    spreads = {}
    factors = {'norm_post_ffn': 4.13, 'lru_ba': 8.0, 'lru_bx': 8.0, 'exp_b1': 8.0, 'exp_b2': 8.0}
    for name, (base, spread) in spreads.items():
        noise = np.random.default_rng([zlib.crc32(name.encode()), seed]).standard_normal(out[name].shape)
        drawn = base * np.exp(spread * noise) if base else spread * noise
        out[name] = __import__('jax').numpy.asarray(drawn.astype(out[name].dtype))
    for name, factor in factors.items():
        out[name] = (out[name] * factor).astype(out[name].dtype)
    return out
```

```python
from contextlib import ExitStack

import numpy as np
import concourse.bass as bass
from concourse import mybir

F32 = mybir.dt.float32
F32R = mybir.dt.float32r
I32 = mybir.dt.int32
U32 = mybir.dt.uint32
ALU = mybir.AluOpType
ACT = mybir.ActivationFunctionType
AX = mybir.AxisListType
ds = bass.ds

P = 128
D = 1024
KT = D // P
SEQ = 256
CTX = 256
TOK = CTX + SEQ
TT = SEQ // P
HEADS = 4
ROW = 64
ROWS = SEQ // ROW
PAD = 8
PROW = ROW + 2 * PAD
CONV = 4
E = 32
TOPK = 4
SLOTS = 64
MORE = 16
ITEMS = E + MORE
EPS = 1e-6
LIMIT = 7.0
ALPHA = 1.702
CHUNK = 256
CW = KT * CHUNK
RING = 4
BANK = 512
CPI = 12
HALF = 512
AHEAD = 4
SPLITS = 6
BLOCK_COL = [0, D, HALF, D + HALF]
POOL_LO = (2, 6, 10)
DVE_LO = tuple(c for c in range(CPI) if c not in POOL_LO)
ARENA = SPLITS * 2 * CW

ROWS1 = [("c", 8), ("c_ctx", 8), ("norm_pre_mix", 8), ("norm_post_mix", 8), ("norm_pre_ffn", 8),
         ("norm_post_ffn", 8), ("b_mod", 48), ("conv_w", 32)]
ROWS2 = [("conv_b", 8), ("lru_ba", 16), ("lru_bx", 16), ("lru_lambda", 16), ("pool_scale", 8)]
COL = {}
for _rows, _base in ((ROWS1, 0), (ROWS2, P)):
    _at = _base
    for _name, _n in _rows:
        COL[_name] = _at
        _at += _n
NVEC = P + 64


def front_plan():
    plan = [("vec", 0, "V")]
    plan += [("mod", c, "V") for c in range(8)]
    plan += [("mt", 0, "V"), ("b1", 0, "V")]
    plan += [("xt", k, "AV"[k % 2]) for k in range(KT)]
    plan += [("xr", j, "A") for j in range(KT)]
    for s in range(2 * HEADS):
        plan += [("lru", s, None), ("xp", s, "A") if s < 4 else ("gg", s - 4, "A")]
    plan += [("mr", c, "A") for c in range(4)] + [("mp", c, "A") for c in range(4)]
    plan += [("pw", g, "A") for g in range(4)]
    for c in range(4):
        plan += [("rp", c, "V"), ("pp", c, "V")]
    plan += [("rs", n, "V") for n in range(8)]
    plan += [("wo", c, "A") for c in range(4)]
    plan += [("vt", n, "AV"[n % 2]) for n in range(4)]
    plan += [("lg", 0, "V"), ("rk", 0, "V"), ("ct", 0, "V")]
    return plan


def build(nc, I, out):
    ctx = ExitStack()
    with ctx:
        def sb(name, shape, dt=F32):
            return ctx.enter_context(nc.sbuf_tensor(name, shape, dt))

        def sem(name):
            return ctx.enter_context(nc.semaphore(name))

        arena_at = -(-nc.sbuf_base // 32) * 32
        arena = sb("arena", [P, ARENA])
        ring = sb("ring", [P, RING * CW])
        bufA = sb("bufA", [P, 4096])
        bufB_at = -(-nc.sbuf_base // 32) * 32
        bufB = sb("bufB", [P, 4096])
        gbuf = sb("gbuf", [P, 2048])
        hbuf = sb("hbuf", [P, 2048])
        m1 = sb("m1", [P, 2048])
        m2 = sb("m2", [P, 2048])
        psum = [ctx.enter_context(nc.psum_tensor(f"bank{b}", [P, BANK], F32)) for b in range(8)]

        ident = sb("ident", [P, P])
        ones = sb("ones", [P, P])
        upper = sb("upper", [P, P])
        iotaI = sb("iotaI", [P, 512], I32)
        slotno = sb("slotno", [P, 512])
        ecol = sb("ecol", [P, 96])
        rcol = sb("rcol", [P, 96])
        jcol = sb("jcol", [P, MORE])
        icnt = sb("icnt", [P, 4 * ROW])
        vstage = sb("vstage", [P, 2 * P])
        vecT = sb("vecT", [P, NVEC])
        modT = sb("modT", [P, 32])
        sT = sb("sT", [P, 2 * KT])
        small = sb("small", [P, 160])
        lamw = sb("lamw", [P, 8 * 16])
        amod = sb("amod", [P, 2 * KT])
        folder = sb("folder", [P, SLOTS])
        stat = sb("stat", [P, 32])
        b1T = sb("b1T", [P, 512])
        rw = sb("rw", [P, KT * E])
        rb = sb("rb", [P, E])
        tabE = sb("tabE", [1, ITEMS], I32)
        tabR = sb("tabR", [1, ITEMS], I32)
        more = sb("more", [1, 1], I32)
        rank = sb("rank", [P, TT * E])
        comb = sb("comb", [P, TT * E])

        xin = bufA[:, :].rearrange("p (t d) -> p t d", t=4)
        xc = bufA[:, :].rearrange("p (j t) -> p j t", j=KT)
        rows = bufA[:, :].rearrange("p (r d) -> p r d", r=4)
        uT = bufB[:, :].rearrange("p (j t) -> p j t", j=KT)
        ypT = bufB[:, 0:2048].rearrange("p (j t) -> p j t", j=KT)
        mgT = bufB[:, 2048:4096].rearrange("p (j t) -> p j t", j=KT)
        gT = gbuf[:, :].rearrange("p (j t) -> p j t", j=KT)
        mlat = gbuf[:, :].rearrange("p (t d) -> p t d", t=TT)
        hT = hbuf[:, :].rearrange("p (j t) -> p j t", j=KT)
        x1 = hbuf[:, :].rearrange("p (t d) -> p t d", t=TT)
        m1T = m1[:, :].rearrange("p (j t) -> p j t", j=KT)
        m2T = m2[:, :].rearrange("p (j t) -> p j t", j=KT)
        vtok = m1[:, :].rearrange("p (t d) -> p t d", t=TT)
        vT = m2[:, :].rearrange("p (j t) -> p j t", j=KT)
        gchunk = [arena[:, n * CW:(n + 1) * CW].rearrange("p (k n) -> p k n", k=KT) for n in range(2)]
        modrow = m1[0:2, :]

        def colsum(q):
            o = 2 * CW + q * CHUNK if q < 8 else 10240 + (q - 8) * CHUNK
            return arena[:, o:o + CHUNK]

        o = 6144
        GP = 2 * ROWS * PROW
        xpp = arena[:, o:o + 4 * GP].rearrange("p (g r q) -> p g r q", g=4, q=PROW)
        winA = arena[:, o + 4 * GP:o + 5 * GP].rearrange("p (r q) -> p r q", q=PROW)
        winB = arena[:, o + 5 * GP:o + 6 * GP].rearrange("p (r q) -> p r q", q=PROW)
        CP = CTX + CONV - 1
        o = 10240
        xrp = arena[:, o:o + KT * 2 * CP].rearrange("p (j s t) -> p j s t", j=KT, s=2)

        def tmp(n):
            a = 16384 + n * 1024
            return arena[:, a:a + 1024].rearrange("p (j t) -> p j t", j=2)
        thr, thi, tnh, dec, rt, amul, bb, hs = (tmp(n) for n in range(8))
        nrow = arena[:, 21504:24576].rearrange("p (r d) -> p r d", r=3)
        def alias(name, n, at):
            return nc.alloc_sbuf_tensor_at(name, [P, n], F32R, offset=at)
        whi = [alias(f"whi{q}", CW, arena_at + 8 * CW * q) for q in range(SPLITS)]
        wlo = [alias(f"wlo{q}", CW, arena_at + 8 * CW * q + 4 * CW) for q in range(SPLITS)]
        whi = [w[:, :].rearrange("p (k n) -> p k n", k=4) for w in whi]
        wlo = [w[:, :].rearrange("p (k n) -> p k n", k=4) for w in wlo]
        RB = bufB
        lg = RB[:, 0:64].rearrange("p (t e) -> p t e", t=TT)
        mx = RB[:, 64:80].rearrange("p (t k) -> p t k", t=TT)
        ixf = RB[:, 80:96].rearrange("p (t k) -> p t k", t=TT)
        ew = RB[:, 96:104].rearrange("p (t k) -> p t k", t=TT)
        mask = RB[:, 128:192].rearrange("p (t e) -> p t e", t=TT)
        oh = RB[:, 192:448].rearrange("p (t k e) -> p t k e", t=TT, k=TOPK)
        ohw = RB[:, 448:704].rearrange("p (t k e) -> p t k e", t=TT, k=TOPK)
        cnt = RB[0:1, 704:736]
        ovr = RB[0:1, 736:832].rearrange("p (r e) -> p r e", r=3)
        ovs = RB[0:1, 832:864]
        inc = RB[0:1, 864:896]
        combT = RB[0:E, 896:1152]
        posr = RB[0:1, 1152:1248].rearrange("p (r e) -> p r e", r=3)
        tabf = RB[0:1, 1248:1344]
        ixu = sb("ixu", [P, 16], U32)
        ojh = m2[0:1, 0:1536].rearrange("p (j q) -> p j q", j=MORE)
        b2s = gbuf[0:E, 0:1024]
        b1stage = m2[:, 1024:1536].rearrange("p (n q) -> p n q", n=4)
        rank_v = rank[:, :].rearrange("p (t e) -> p t e", t=TT)
        comb_v = comb[:, :].rearrange("p (t e) -> p t e", t=TT)
        sel = bufB[:, 1408:1536].rearrange("p (t c) -> p t c", t=TT)
        selw = bufB[:, 1536:1792].rearrange("p (t c) -> p t c", t=TT)
        gt = bufB[:, 1792:2048]
        xhl = alias("xhl", 1024, bufB_at + 4 * 2048)[:, :].rearrange("p (k q c) -> p k q c", k=KT, q=2)
        ahl = alias("ahl", 1024, bufB_at + 4 * 3072)[:, :].rearrange("p (k q c) -> p k q c", k=KT, q=2)
        zS = [gbuf[:, 1024 + q * 512:1536 + q * 512] for q in range(2)]
        yS = m2[:, 0:1024]
        glu, lin, sg, actf = (m2[:, 1024 + q * 256:1280 + q * 256] for q in range(4))

        ring_landed = [sem(f"ring_landed{r}") for r in range(RING)]
        vecs_landed, tokens_landed, late_landed = sem("vecs_landed"), sem("tokens_landed"), sem("late_landed")
        xres_landed = sem("xres_landed")
        hi_done, lo_dve, lo_pool = sem("hi_done"), sem("lo_dve"), sem("lo_pool")
        w_used = sem("w_used")
        gmod_landed = [sem(f"gmod_landed{n}") for n in range(2)]
        sums_ready, brow_landed, nrow_landed, rows_ready = sem("sums_ready"), sem("brow_landed"), sem("nrow_landed"), sem("rows_ready")
        z_ready, fold_done, xlo_ready, ahi_ready, alo_ready = (
            sem(n) for n in ("z_ready", "fold_done", "xlo_ready", "ahi_ready", "alo_ready"))
        out_written = sem("out_written")
        consts_ready, pads_ready = sem("consts_ready"), sem("pads_ready")
        job_done = sem("job_done")
        read_act, read_dve = sem("read_act"), sem("read_dve")
        ssq_ready, rstd_var, rstd_root, tok_scaled = sem("ssq_ready"), sem("rstd_var"), sem("rstd_root"), sem("tok_scaled")
        silu_th, silu_ready = sem("silu_th"), sem("silu_ready")
        lam_abs, lam_exp, lru_consts = sem("lam_abs"), sem("lam_exp"), sem("lru_consts")
        mod_ready = sem("mod_ready")
        conv_done = sem("conv_done")
        gates_done, gates_read, coef_ready, lru_done = sem("gates_done"), sem("gates_read"), sem("coef_ready"), sem("lru_done")
        gelu_ready, yrnn_ready, pool_ready = sem("gelu_ready"), sem("yrnn_ready"), sem("pool_ready")
        merged_ready = sem("merged_ready")
        ssq2_ready, var2, root2, x1_ready, v_ready, ssq3_ready, var3, root3 = (
            sem(n) for n in ("ssq2_ready", "var2", "root2", "x1_ready", "v_ready", "ssq3_ready", "var3", "root3"))
        neg_max, exps_ready, mask_ready, comb_ready = (
            sem(n) for n in ("neg_max", "exps_ready", "mask_ready", "comb_ready"))
        acc_init, items_ready = sem("acc_init"), sem("items_ready")
        sel_ready, selw_ready, gather_done, xhi_ready = sem("sel_ready"), sem("selw_ready"), sem("gather_done"), sem("xhi_ready")
        glu_ready, sig_ready, act_ready = sem("glu_ready"), sem("sig_ready"), sem("act_ready")
        gt_done, gt_ready, y_ready, scatter_done = (
            sem(n) for n in ("gt_done", "gt_ready", "y_ready", "scatter_done"))
        ssq4_ready, var4, root4, out_ready = sem("ssq4_ready"), sem("var4"), sem("root4"), sem("out_ready")
        act_chain, dve_chain, pool_chain, tail_chain = sem("act_chain"), sem("dve_chain"), sem("pool_chain"), sem("tail_chain")

        plan = front_plan()
        number, reads = {}, {"A": 0, "V": 0}
        read_at = []
        for kind, n, reader in plan:
            if kind == "lru":
                continue
            number[kind, n] = len(read_at)
            reads[reader] += 1
            read_at.append((reader, reads[reader]))
        JOBS = len(read_at)

        def bank_of(kind, n):
            return psum[4 + number[kind, n] % 4]

        def cols(w, c):
            return w[:, c * CHUNK:(c + 1) * CHUNK].rearrange("(k p) n -> p k n", p=P)

        w_in, w_mod = I["w_in"][0], I["w_mod"][0]
        ROW_GROUP = [2, 4, 3, 5]
        chunks, chunk_no = [], {}
        for kind, n, _ in plan:
            c = None
            if kind == "mod":
                c = [(cols(w_mod, n), 0)]
            elif kind == "xr" and n % 2 == 0:
                c = [(cols(w_in, n // 2), 0)]
            elif kind == "lru":
                h, d = n // 2, n % 2
                c = [(I[w][0, d, h].rearrange("(k p) n -> p k n", p=P), q * 512)
                     for q, w in enumerate(("lru_wa", "lru_wx"))]
            elif kind in ("gg", "xp", "mr", "mp"):
                c = [(cols(w_in, {"gg": 4, "xp": 8, "mr": 12, "mp": 16}[kind] + n), 0)]
            elif kind == "pw" and n == 0:
                c = [(I["pool_w"][0].rearrange("g (k p) n -> p g k n", p=P), 0)]
            elif kind in ("rp", "pp", "wo"):
                c = [(cols(I[{"rp": "w_rnn_proj", "pp": "w_pool_proj", "wo": "w_out"}[kind]][0], n), 0)]
            if c:
                chunk_no[kind, n] = len(chunks)
                chunks.append(c)
        landed, per = [], [0] * RING
        for n, c in enumerate(chunks):
            per[n % RING] += 16 * len(c)
            landed.append(per[n % RING])

        def chunk_of(kind, n):
            r = chunk_no[kind, n] % RING
            return ring[:, r * CW:(r + 1) * CW]

        def chunk_used(n):
            kind, m = next(key for key, c in chunk_no.items() if c == n)
            if kind == "lru":
                return gates_done, m + 1
            if kind in ("xr", "pw"):
                m += {"xr": 1, "pw": 3}[kind]
            return job_done, number[kind, m] + 1

        NF = len(chunks)

        def raw(c):
            r = (NF + c) % RING
            return ring[:, r * CW:(r + 1) * CW], ring_landed[r], per[r]

        def raw_wait(eng, i, c):
            _, landed_sem, base = raw(c)
            eng.wait_ge(landed_sem, i * (16 * CPI // RING) + (base + 16 * (c // RING + 1)))

        def lo_wait(eng, i, c):
            if c in POOL_LO:
                eng.wait_ge(lo_pool, i * len(POOL_LO) + (POOL_LO.index(c) + 1))
            else:
                eng.wait_ge(lo_dve, i * len(DVE_LO) + (DVE_LO.index(c) + 1))

        def block_of(c):
            return (c // 2, c % 2) if c < 8 else (4 + c % 2, (c - 8) // 2)

        def expert_src(e, c):
            b, q = block_of(c)
            w, col = (I["exp_w1"], BLOCK_COL[b]) if b < 4 else (I["exp_w2"], (b - 4) * HALF)
            return w[0, ds(e, 1), q * 512:(q + 1) * 512, col:col + HALF].rearrange("a (k p) n -> p (a k) n", p=P)

        def xrows(src):
            return src.broadcast_to([P, src.shape[-1]])

        block = ctx.enter_context(nc.Block())

        @block.sync
        def _(sp):
            def load_raw(e, c):
                dst, landed_sem, _ = raw(c)
                sp.dma_start(dst.rearrange("p (k n) -> p k n", k=4), expert_src(e, c)).then_inc(landed_sem, 16)

            for n, parts in enumerate(chunks):
                if n >= RING:
                    sp.wait_ge(*chunk_used(n - RING))
                for src, o in parts:
                    r = (n % RING) * CW + o
                    w = int(np.prod(src.shape)) // P
                    dst = ring[:, r:r + w]
                    if len(src.shape) == 4:
                        dst = dst.rearrange("p (g k n) -> p g k n", g=src.shape[1], k=src.shape[2])
                    else:
                        dst = dst.rearrange("p (k n) -> p k n", k=src.shape[1])
                    sp.dma_start(dst, src).then_inc(ring_landed[n % RING], 16)
                if n == chunk_no["mp", 0]:
                    sp.wait_ge(lru_done, 2 * HEADS)
                    for r, g in enumerate(ROW_GROUP):
                        sp.dma_start(rows[:, r, :], xrows(I["b_mod"][0:1, g * D:(g + 1) * D])).then_inc(brow_landed, 16)
                    for r, name in enumerate(("norm_post_mix", "norm_pre_ffn", "norm_post_ffn")):
                        sp.dma_start(nrow[:, r, :], xrows(I[name])).then_inc(nrow_landed, 16)
                if n == chunk_no["rp", 0]:
                    sp.wait_ge(yrnn_ready, 1)
                    sp.dma_start(x1, I["x"][0].rearrange("(t p) d -> p t d", p=P)).then_inc(xres_landed, 16)
            for c in range(CPI):
                if c < RING:
                    sp.wait_ge(*chunk_used(NF + c - RING))
                else:
                    lo_wait(sp, 0, c - RING)
                load_raw(0, c)
            sp.wait_ge(items_ready, 1)
            last_item = sp.value_load(more[0:1, 0:1], min_val=0, max_val=MORE - 1) + (E - 1)
            with sp.Fori(1, last_item + 1) as i:
                e = sp.value_load(tabE[0:1, ds(i, 1)], min_val=0, max_val=E - 1)
                for c in range(CPI):
                    lo_wait(sp, i if c >= RING else i - 1, (c - RING) % CPI)
                    load_raw(e, c)
            for t in range(TT):
                sp.wait_ge(out_ready, t + 1)
                sp.dma_start(out[0, t * P:(t + 1) * P, :], x1[:, t, :]).then_inc(out_written, 16)
            sp.wait_ge(out_written, 16 * TT)

        @block.gpsimd
        def _(pool):
            g = nc.gpsimd
            chain = [0]

            def link(ins):
                chain[0] += 1
                ins.then_inc(pool_chain, 1)
                pool.wait_ge(pool_chain, chain[0])

            pool.dma_start(xin[:, 0:2, :], I["ctx"][0].rearrange("(t p) d -> p t d", p=P)).then_inc(tokens_landed, 16)
            pool.dma_start(xin[:, 2:4, :], I["x"][0].rearrange("(t p) d -> p t d", p=P)).then_inc(tokens_landed, 16)
            g.memset(ident[:, :], 0.0)
            g.memset(upper[:, :], 1.0)
            link(g.memset(ones[:, :], 1.0))
            g.affine_select(out=ident[:, :], in_=ident[:, :], compare_op=ALU.not_equal, fill=1.0, base=0,
                            pattern=[[-1, P]], channel_multiplier=1)
            g.affine_select(out=upper[:, :], in_=upper[:, :], compare_op=ALU.is_gt, fill=0.0, base=0,
                            pattern=[[1, P]], channel_multiplier=-1).then_inc(consts_ready, 1)
            pool.wait_ge(consts_ready, 1)
            g.tensor_tensor(folder[:, :], ident[:, 0:SLOTS], ident[:, SLOTS:P], ALU.add)
            g.memset(xrp[:, :, :, 0:2], 0.0)
            g.memset(xrp[:, :, :, CP - 1:CP], 0.0)
            xz = xpp[:, :, :, :].rearrange("p g r q -> p (g r) q")
            g.memset(xz[:, :, 0:PAD], 0.0)
            g.memset(xz[:, :, PAD + ROW:PROW], 0.0).then_inc(pads_ready, 1)
            link(g.iota(iotaI[:, :], pattern=[[64, 4], [0, 2], [1, 64]], base=0, channel_multiplier=0))
            link(g.tensor_copy(slotno[:, :], iotaI[:, :]))
            link(g.iota(iotaI[:, 0:96], pattern=[[0, 3], [1, 32]], base=0, channel_multiplier=0))
            link(g.tensor_copy(ecol[:, :], iotaI[:, 0:96]))
            link(g.iota(iotaI[:, 0:96], pattern=[[1, 3], [0, 32]], base=1, channel_multiplier=0))
            link(g.tensor_copy(rcol[:, :], iotaI[:, 0:96]))
            link(g.iota(iotaI[:, 0:MORE], pattern=[[1, MORE]], base=1, channel_multiplier=0))
            g.tensor_copy(jcol[:, :], iotaI[:, 0:MORE]).then_inc(consts_ready, 1)

            def gmod_load(q):
                c = ROW_GROUP[q // 4] * 4 + q % 4
                pool.dma_start(gchunk[q % 2], cols(w_mod, c)).then_inc(gmod_landed[q % 2], 16)

            def gmod_sum(q):
                w = gchunk[q % 2]
                pool.wait_ge(gmod_landed[q % 2], 16 * (q // 2 + 1))
                sb_ = sT[:, :].rearrange("p (k s) -> p k s", s=2)[:, :, 0:1].broadcast_to([P, KT, CHUNK])
                link(g.tensor_tensor(w, w, sb_, ALU.mult))
                link(g.tensor_tensor(w[:, 0:4], w[:, 0:4], w[:, 4:8], ALU.add))
                link(g.tensor_tensor(w[:, 0:2], w[:, 0:2], w[:, 2:4], ALU.add))
                g.tensor_tensor(colsum(q), w[:, 0], w[:, 1], ALU.add).then_inc(sums_ready, 1)
                pool.wait_ge(sums_ready, q + 1)
                if q + 2 < 16:
                    gmod_load(q + 2)

            gmod_load(0)
            gmod_load(1)
            pool.wait_ge(silu_ready, 1)
            for q in range(8):
                gmod_sum(q)
            for gi in range(4):
                pool.wait_ge(read_act, read_at[number["xp", gi]][1])
                x = xpp[:, gi]
                a, b = winA, winB
                link(g.tensor_tensor(a[:, :, 1:80], x[:, :, 0:79], x[:, :, 1:80], ALU.add))
                if gi >= 1:
                    link(g.tensor_tensor(b[:, :, 2:79], a[:, :, 1:78], a[:, :, 3:80], ALU.add))
                    a, b = b, a
                if gi >= 2:
                    link(g.tensor_tensor(b[:, :, 4:77], a[:, :, 2:75], a[:, :, 6:79], ALU.add))
                    a, b = b, a
                if gi >= 3:
                    link(g.tensor_tensor(b[:, :, 8:72], a[:, :, 4:68], a[:, :, 12:76], ALU.add))
                    a, b = b, a
                if gi == 0:
                    pool.wait_ge(consts_ready, 3)
                inv = icnt[:, gi * ROW:(gi + 1) * ROW].rearrange("p (a q) -> p a q", a=1).broadcast_to(
                    [P, 2 * ROWS, ROW])
                xs = x[:, :, PAD:PAD + ROW]
                link(g.tensor_tensor(a[:, :, 8:72], a[:, :, 8:72], inv, ALU.mult))
                g.tensor_tensor(xs, a[:, :, 8:72], xs, ALU.subtract).then_inc(pool_ready, 1)
                pool.wait_ge(pool_ready, gi + 1)
            pool.wait_ge(conv_done, KT)
            for q in range(8, 16):
                gmod_sum(q)

            def make_lo(i, c):
                raw_ap, _, _ = raw(c)
                pool.wait_ge(hi_done, i * CPI + (c + 1))
                g.tensor_tensor(wlo[c % SPLITS].rearrange("p k n -> p (k n)"), raw_ap,
                                whi[c % SPLITS].rearrange("p k n -> p (k n)").bitcast(F32),
                                ALU.subtract).then_inc(lo_pool, 1)

            for c in POOL_LO:
                make_lo(0, c)
            pool.wait_ge(items_ready, 1)
            last_item = pool.value_load(more[0:1, 0:1], min_val=0, max_val=MORE - 1) + (E - 1)
            with pool.Fori(1, last_item + 1) as i:
                for c in POOL_LO:
                    make_lo(i, c)

        @block.tensor
        def _(pe):
            mm = nc.tensor.matmul
            job = [0]

            def start_job():
                m = job[0]
                if m >= 4:
                    reader, count = read_at[m - 4]
                    pe.wait_ge(read_act if reader == "A" else read_dve, count)
                return psum[4 + m % 4]

            def end_job(ins):
                job[0] += 1
                ins.then_inc(job_done, 1)

            def arrive(kind, n):
                c = chunk_no[kind, n]
                pe.wait_ge(ring_landed[c % RING], landed[c])
                return chunk_of(kind, n)

            pe.wait_ge(consts_ready, 1)
            pe.wait_ge(vecs_landed, 16 * 13)
            for kind, n, _ in plan:
                if kind == "lru":
                    h, d = n // 2, n % 2
                    w = arrive("lru", n)[:, 0:1024].rearrange("p (q k n) -> p q k n", q=2, k=2)
                    if d == 0:
                        pe.wait_ge(conv_done, 2 * h + 2)
                    if n:
                        pe.wait_ge(gates_read, n)
                    for q in range(2):
                        for j in range(2):
                            for k in range(2):
                                last = mm(psum[2 * q + j][:, :], w[:, q, k, j * P:(j + 1) * P],
                                          xc[:, 2 * h + k, :], start=(k == 0), stop=(k == 1))
                    last.then_inc(gates_done, 1)
                    continue
                if kind == "xt" and n == 0:
                    pe.wait_ge(tok_scaled, 4)
                if kind == "xr" and n == 0:
                    pe.wait_ge(read_act, read_at[number["xt", KT - 2]][1])
                    pe.wait_ge(read_dve, read_at[number["xt", KT - 1]][1])
                if kind == "mod" and n == 0:
                    pe.wait_ge(silu_ready, 1)
                b = start_job()
                if kind == "vec":
                    nc.tensor.transpose(b[:, 0:P], vstage[:, 0:P], ident[:, :])
                    end_job(nc.tensor.transpose(b[:, P:P + 64], vstage[0:64, P:2 * P], ident[0:64, 0:64]))
                elif kind == "b1":
                    pe.wait_ge(late_landed, 16 * 3)
                    for q in range(4):
                        last = nc.tensor.transpose(b[:, q * P:(q + 1) * P], b1stage[:, q, :], ident[:, :])
                    end_job(last)
                elif kind == "mod":
                    w = arrive("mod", n).rearrange("p (k n) -> p k n", k=KT)
                    for k in range(KT):
                        last = mm(b[0:2, 0:CHUNK], sT[:, 2 * k:2 * k + 2], w[:, k, :], start=(k == 0), stop=(k == KT - 1))
                    end_job(last)
                elif kind == "mt":
                    pe.wait_ge(read_dve, read_at[number["mod", 7]][1])
                    for j in range(16):
                        last = nc.tensor.transpose(b[:, 2 * j:2 * j + 2], modrow[:, j * P:(j + 1) * P], ident[0:2, 0:2])
                    end_job(last)
                elif kind == "xt":
                    for t in range(4):
                        last = nc.tensor.transpose(b[:, t * P:(t + 1) * P], xin[:, t, n * P:(n + 1) * P], ident[:, :])
                    end_job(last)
                elif kind == "xr":
                    w = arrive("xr", n - n % 2).rearrange("p (k n) -> p k n", k=KT)
                    j = n % 2
                    for k in range(KT):
                        last = mm(b[:, :], w[:, k, j * P:(j + 1) * P], uT[:, k, :], start=(k == 0), stop=(k == KT - 1))
                    end_job(last)
                elif kind in ("xp", "gg", "mr", "mp", "rp", "pp"):
                    if kind == "rp" and n == 0:
                        pe.wait_ge(yrnn_ready, 1)
                    if kind == "pp" and n == 0:
                        pe.wait_ge(read_act, read_at[number["pw", 3]][1])
                    w = arrive(kind, n).rearrange("p (k n) -> p k n", k=KT)
                    src = {"rp": gT, "pp": ypT}.get(kind, uT[:, :, CTX:TOK])
                    for j in range(2):
                        for k in range(KT):
                            last = mm(b[:, j * SEQ:(j + 1) * SEQ], w[:, k, j * P:(j + 1) * P], src[:, k, :],
                                      start=(k == 0), stop=(k == KT - 1))
                    end_job(last)
                elif kind == "pw":
                    if n == 0:
                        pe.wait_ge(pool_ready, 4)
                        arrive("pw", 0)
                    w = chunk_of("pw", 0).rearrange("p (g k n) -> p g k n", g=4, k=2)
                    for j in range(2):
                        for k in range(2):
                            last = mm(b[:, j * SEQ:(j + 1) * SEQ], w[:, n, k, j * P:(j + 1) * P],
                                      xpp[:, n, k * ROWS:(k + 1) * ROWS, PAD:PAD + ROW], start=(k == 0), stop=(k == 1))
                    end_job(last)
                elif kind == "rs":
                    pe.wait_ge(sums_ready, 2 * n + 2)
                    for q in range(2):
                        last = mm(b[:, q * CHUNK:(q + 1) * CHUNK], ones[:, :], colsum(2 * n + q), start=True, stop=True)
                    end_job(last)
                elif kind == "wo":
                    w = arrive("wo", n).rearrange("p (k n) -> p k n", k=KT)
                    if n == 0:
                        pe.wait_ge(merged_ready, 4)
                    for t in range(TT):
                        for k in range(KT):
                            last = mm(b[:, t * CHUNK:(t + 1) * CHUNK], mgT[:, k, t * P:(t + 1) * P], w[:, k, :],
                                      start=(k == 0), stop=(k == KT - 1))
                    end_job(last)
                elif kind == "vt":
                    if n == 0:
                        pe.wait_ge(v_ready, TT)
                    for kk in range(2):
                        for t in range(TT):
                            k = 2 * n + kk
                            last = nc.tensor.transpose(b[:, kk * SEQ + t * P:kk * SEQ + (t + 1) * P],
                                                       vtok[:, t, k * P:(k + 1) * P], ident[:, :])
                    end_job(last)
                elif kind == "lg":
                    pe.wait_ge(read_act, read_at[number["vt", 2]][1])
                    pe.wait_ge(read_dve, read_at[number["vt", 3]][1])
                    for t in range(TT):
                        for k in range(KT):
                            last = mm(b[:, t * E:(t + 1) * E], vT[:, k, t * P:(t + 1) * P], rw[:, k * E:(k + 1) * E],
                                      start=(k == 0), stop=(k == KT - 1))
                    end_job(last)
                elif kind == "rk":
                    pe.wait_ge(mask_ready, 1)
                    mm(b[:, 0:E], upper[:, :], mask[:, 0, :], start=True, stop=True)
                    mm(b[:, E:2 * E], upper[:, :], mask[:, 1, :], start=True, stop=False)
                    mm(b[:, E:2 * E], ones[:, :], mask[:, 0, :], start=False, stop=True)
                    mm(b[:, 2 * E:3 * E], ones[:, :], mask[:, 0, :], start=True, stop=False)
                    end_job(mm(b[:, 2 * E:3 * E], ones[:, :], mask[:, 1, :], start=False, stop=True))
                elif kind == "ct":
                    pe.wait_ge(comb_ready, 1)
                    for t in range(TT):
                        last = nc.tensor.transpose(b[0:E, t * P:(t + 1) * P], comb_v[:, t, :], ident[:, :])
                    end_job(last)

            for reader, count in read_at[JOBS - 4:]:
                pe.wait_ge(read_act if reader == "A" else read_dve, count)
            pe.wait_ge(gates_read, 2 * HEADS)
            pe.wait_ge(late_landed, 16 * 4)

            def gather():
                for k in range(KT):
                    for t in range(TT):
                        last = mm(psum[7][:, k * SLOTS:(k + 1) * SLOTS], vtok[:, t, k * P:(k + 1) * P], sel[:, t, :],
                                  start=(t == 0), stop=(t == TT - 1))
                last.then_inc(gather_done, 1)

            def chunk(i, c, stat):
                if c < CPI:
                    b, q = block_of(c)
                    pe.wait_ge(hi_done, i * CPI + (c + 1))
                    lo_wait(pe, i, c)
                    for k in range(4):
                        lhs = stat[:, 4 * q + k].rearrange("p q c -> p (q c)")
                        for w in (whi, wlo):
                            last = mm(psum[4 + b % 2][:, :], lhs, w[c % SPLITS][:, k, :],
                                      start=(q == 0 and k == 0 and w is whi), stop=(q == 1 and k == 3 and w is wlo))
                    last.then_inc(w_used, 1)

            def fold(i, b):
                pe.wait_ge(z_ready, i * 4 + (b + 1))
                o = (b % 2) * 256
                for f in range(4):
                    last = mm(psum[6][:, o + f * SLOTS:o + (f + 1) * SLOTS], zS[b % 2][:, f * P:(f + 1) * P],
                              folder[:, :], start=True, stop=True)
                last.then_inc(fold_done, 1)

            def spread():
                for t in range(TT):
                    last = nc.tensor.transpose(psum[7][:, t * P:(t + 1) * P], selw[:, t, :], ident[:, :])
                last.then_inc(gt_done, 1)

            def scatter():
                for t in range(TT):
                    for half in range(2):
                        last = mm(psum[2 * t + half][:, :], gt[:, t * P:(t + 1) * P], yS[:, half * 512:(half + 1) * 512],
                                  start=False, stop=False, skip_group_check=True)
                last.then_inc(scatter_done, 1)

            def item(i, first=False, last=False):
                pe.wait_ge(xhi_ready, i + 1)
                pe.wait_ge(xlo_ready, i + 1)
                if not first:
                    pe.wait_ge(y_ready, i * 2 - 1)
                chunk(i, 0, xhl)
                chunk(i, 1, xhl)
                if not first:
                    pe.wait_ge(y_ready, i * 2)
                chunk(i, 2, xhl)
                chunk(i, 3, xhl)
                fold(i, 0)
                if not first:
                    scatter()
                pe.wait_ge(selw_ready, i + 1)
                spread()
                chunk(i, 4, xhl)
                chunk(i, 5, xhl)
                pe.wait_ge(glu_ready, i * 2 + 1)
                fold(i, 1)
                chunk(i, 6, xhl)
                chunk(i, 7, xhl)
                pe.wait_ge(act_ready, i * 2 + 1)
                fold(i, 2)
                pe.wait_ge(ahi_ready, i * 2 + 1)
                pe.wait_ge(alo_ready, i * 2 + 1)
                chunk(i, 8, ahl)
                pe.wait_ge(glu_ready, i * 2 + 2)
                fold(i, 3)
                chunk(i, 9, ahl)
                if not last:
                    pe.wait_ge(sel_ready, i + 2)
                    pe.wait_ge(gt_ready, i + 1)
                    gather()
                pe.wait_ge(ahi_ready, i * 2 + 2)
                pe.wait_ge(alo_ready, i * 2 + 2)
                chunk(i, 10, ahl)
                chunk(i, 11, ahl)

            pe.wait_ge(sel_ready, 1)
            gather()
            pe.wait_ge(read_dve, read_at[number["ct", 0]][1])
            for t in range(TT):
                for half in range(2):
                    last = mm(psum[2 * t + half][:, :], combT[:, t * P:(t + 1) * P], b2s[:, half * 512:(half + 1) * 512],
                              start=True, stop=False, skip_group_check=True)
            last.then_inc(acc_init, 1)
            item(0, first=True)
            pe.wait_ge(items_ready, 1)
            last_item = pe.value_load(more[0:1, 0:1], min_val=0, max_val=MORE - 1) + (E - 1)
            with pe.Fori(1, last_item) as i:
                item(i)
            item(last_item, last=True)
            pe.wait_ge(y_ready, last_item * 2 + 2)
            pe.wait_ge(gt_ready, last_item + 1)
            scatter()

        @block.scalar
        def _(act):
            a = nc.scalar
            for name, n in ROWS1 + ROWS2:
                src = I[name]
                while len(src.shape) > 1:
                    src = src.rearrange({2: "a b -> (a b)", 3: "a b c -> (a b c)"}[len(src.shape)])
                src = src.rearrange("(r q) -> r q", q=P)
                c = COL[name]
                o = c // P * P
                act.dma_start(vstage[c - o:c - o + n, o:o + P], src).then_inc(vecs_landed, 16)
            act.dma_start(b1stage, I["exp_b1"][0].rearrange("e (f q) -> (e f) q", q=P).rearrange(
                "(n r) q -> r n q", r=P)).then_inc(late_landed, 16)
            act.dma_start(rw[:, :].rearrange("p (k e) -> p k e", k=KT),
                          I["router_w"][0].rearrange("(k p) e -> p k e", p=P)).then_inc(late_landed, 16)
            act.dma_start(rb[:, :], I["router_b"].broadcast_to([P, E])).then_inc(late_landed, 16)
            chain = [0]

            def link(ins):
                chain[0] += 1
                ins.then_inc(act_chain, 1)
                act.wait_ge(act_chain, chain[0])

            def job_of(kind, n):
                act.wait_ge(job_done, number[kind, n] + 1)
                return bank_of(kind, n)

            act.wait_ge(read_dve, 1)
            a.activation(small[:, 0:16], vecT[:, 0:16], ACT.Tanh, scale=0.5).then_inc(silu_th, 1)
            act.wait_ge(lam_abs, 1)
            a.activation(lamw[:, 16:32], lamw[:, 0:16], ACT.Exp, scale=-1.0).then_inc(lam_exp, 1)
            act.wait_ge(tokens_landed, 32)
            for t in range(4):
                ins = a.activation(arena[:, 16384:16384 + D], xin[:, t, :], ACT.Square, accum_out=stat[:, t:t + 1])
                ins.then_inc(ssq_ready, 1)
                act.wait_ge(ssq_ready, t + 1)
            act.wait_ge(rstd_var, 1)
            a.activation(stat[:, 8:12], stat[:, 4:8], ACT.Sqrt).then_inc(rstd_root, 1)

            act.wait_ge(mod_ready, 1)
            for k in range(0, KT, 2):
                b = job_of("xt", k)
                for s in range(2):
                    m = 1 - s
                    ins = a.activation(uT[:, k, s * CTX:(s + 1) * CTX], b[:, s * CTX:(s + 1) * CTX], ACT.Identity,
                                       bias=modT[:, 2 * k + m:2 * k + m + 1], scale=amod[:, 2 * k + m:2 * k + m + 1])
                ins.then_inc(read_act, 1)
            act.wait_ge(pads_ready, 1)
            for j in range(KT):
                b = job_of("xr", j)
                a.activation(xrp[:, j, :, 2:2 + CTX], b[:, :].rearrange("p (s t) -> p s t", s=2),
                             ACT.Copy).then_inc(read_act, 1)
            act.wait_ge(lru_consts, 1)
            for s in range(2 * HEADS):
                h, d = s // 2, s % 2
                act.wait_ge(gates_done, s + 1)
                if s:
                    act.wait_ge(lru_done, s)
                for j in range(2):
                    c = d * KT + 2 * h + j
                    a.activation(thr[:, j, :], psum[j][:, :], ACT.Tanh, bias=lamw[:, 64 + c:65 + c], scale=0.5)
                    ins = a.activation(thi[:, j, :], psum[2 + j][:, :], ACT.Tanh, bias=lamw[:, 80 + c:81 + c], scale=0.5)
                ins.then_inc(gates_read, 1)
                act.wait_ge(gates_read, s + 1)
                for j in range(2):
                    c = d * KT + 2 * h + j
                    a.activation(tnh[:, j, :], thr[:, j, :], ACT.Tanh, bias=lamw[:, 96 + c:97 + c],
                                 scale=lamw[:, 96 + c:97 + c])
                    ins = a.activation(dec[:, j, :], thr[:, j, :], ACT.Exp, bias=lamw[:, 112 + c:113 + c],
                                       scale=lamw[:, 112 + c:113 + c])
                link(ins)
                a.activation(rt, tnh, ACT.Sqrt).then_inc(coef_ready, 1)
                if s < 4:
                    b = job_of("xp", s)
                    ins = a.activation(xpp[:, s, :, PAD:PAD + ROW], b[:, :].rearrange("p (r q) -> p r q", q=ROW), ACT.Copy)
                    ins.then_inc(read_act, 1)
                else:
                    b = job_of("gg", s - 4)
                    a.activation(gbuf[:, (s - 4) * 512:(s - 3) * 512], b[:, :], ACT.Copy).then_inc(read_act, 1)
            act.wait_ge(read_act, read_at[number["gg", 3]][1])
            a.activation(gbuf[:, :], gbuf[:, :], ACT.Gelu_apprx_tanh).then_inc(gelu_ready, 1)
            for kind, dst in (("mr", m1), ("mp", m2)):
                for c in range(4):
                    b = job_of(kind, c)
                    a.activation(dst[:, c * 512:(c + 1) * 512], b[:, :], ACT.Tanh, scale=0.5).then_inc(read_act, 1)
            for gi in range(4):
                b = job_of("pw", gi)
                for j in range(2):
                    c = COL["pool_scale"] + 2 * gi + j
                    ins = a.activation(ypT[:, 2 * gi + j, :], b[:, j * SEQ:(j + 1) * SEQ], ACT.Copy,
                                       scale=vecT[:, c:c + 1])
                ins.then_inc(read_act, 1)

            def make_hi(i, c, used=True):
                raw_ap, _, _ = raw(c)
                raw_wait(act, i, c)
                if used and not (isinstance(i, int) and i * CPI + c < SPLITS):
                    act.wait_ge(w_used, i * CPI + (c + 1 - SPLITS))
                a.activation(whi[c % SPLITS].rearrange("p k n -> p (k n)"), raw_ap, ACT.Copy).then_inc(hi_done, 1)

            act.wait_ge(job_done, number["rp", 3] + 1)
            for c in range(4):
                b = job_of("wo", c)
                ins = a.activation(mlat[:, :, c * CHUNK:(c + 1) * CHUNK], b[:, :].rearrange("p (t n) -> p t n", t=TT),
                                   ACT.Copy, scale=0.5)
                ins.then_inc(read_act, 1)
                act.wait_ge(read_act, read_at[number["wo", c]][1])
                for t in range(TT):
                    a.activation(bufB[:, t * CHUNK:(t + 1) * CHUNK], mlat[:, t, c * CHUNK:(c + 1) * CHUNK], ACT.Square,
                                 accum_out=small[:, 64 + 4 * t + c:65 + 4 * t + c]).then_inc(ssq2_ready, 1)
                act.wait_ge(ssq2_ready, 2 * c + 2)
                if c == 2:
                    make_hi(0, 0, used=False)
            act.wait_ge(var2, 1)
            a.activation(stat[:, 16:18], stat[:, 14:16], ACT.Sqrt).then_inc(root2, 1)
            make_hi(0, 1, used=False)
            for t in range(TT):
                act.wait_ge(x1_ready, t + 1)
                a.activation(bufB[:, t * D:(t + 1) * D], x1[:, t, :], ACT.Square,
                             accum_out=stat[:, 20 + t:21 + t]).then_inc(ssq3_ready, 1)
            act.dma_start(b2s, I["exp_b2"][0]).then_inc(late_landed, 16)
            act.wait_ge(var3, 1)
            a.activation(stat[:, 24:26], stat[:, 22:24], ACT.Sqrt).then_inc(root3, 1)
            for c in range(2, min(4, AHEAD)):
                make_hi(0, c, used=False)
            for n in (0, 2):
                b = job_of("vt", n)
                ins = a.activation(m2[:, n * 512:(n + 1) * 512], b[:, :], ACT.Copy)
                ins.then_inc(read_act, 1)
            for c in range(4, AHEAD):
                make_hi(0, c, used=False)
            act.wait_ge(neg_max, 1)
            for t in range(TT):
                a.activation(ew[:, t, :], mx[:, t, 0:TOPK], ACT.Exp, bias=stat[:, 28 + t:29 + t],
                             accum_out=stat[:, 30 + t:31 + t]).then_inc(exps_ready, 1)

            def take_tokens(n):
                act.wait_ge(gather_done, n)
                a.activation(xhl[:, :, 0, :], psum[7][:, :].rearrange("p (k c) -> p k c", k=KT),
                             ACT.Copy).then_inc(xhi_ready, 1)

            def take_block(i, c):
                b, _ = block_of(c)
                act.wait_ge(w_used, i * CPI + (c + 1))
                dst = zS[b % 2] if b < 4 else yS[:, (b - 4) * 512:(b - 3) * 512]
                a.activation(dst, psum[4 + b % 2][:, :], ACT.Copy).then_inc(z_ready if b < 4 else y_ready, 1)

            def sigmoid(i, p):
                act.wait_ge(glu_ready, i * 2 + (p + 1))
                a.activation(sg, glu, ACT.Sigmoid, scale=ALPHA).then_inc(sig_ready, 1)

            def act_hi(i, p):
                act.wait_ge(act_ready, i * 2 + (p + 1))
                a.activation(ahl[:, 4 * p:4 * p + 4, 0, :], actf.rearrange("p (f c) -> p f c", f=4),
                             ACT.Copy).then_inc(ahi_ready, 1)

            def item(i, last=False):
                def ahead(c):
                    n = c + AHEAD
                    if n < CPI:
                        make_hi(i, n)
                    elif not last:
                        make_hi(i + 1, n - CPI)

                ahead(0)
                ahead(1)
                take_block(i, 1)
                ahead(2)
                ahead(3)
                take_block(i, 3)
                sigmoid(i, 0)
                act.wait_ge(gt_done, i + 1)
                a.activation(gt, psum[7][:, 0:SEQ], ACT.Copy).then_inc(gt_ready, 1)
                ahead(4)
                ahead(5)
                take_block(i, 5)
                act_hi(i, 0)
                ahead(6)
                ahead(7)
                take_block(i, 7)
                sigmoid(i, 1)
                ahead(8)
                act_hi(i, 1)
                if not last:
                    take_tokens(i + 2)
                ahead(9)
                ahead(10)
                take_block(i, 10)
                ahead(11)
                take_block(i, 11)

            take_tokens(1)
            item(0)
            act.wait_ge(items_ready, 1)
            last_item = act.value_load(more[0:1, 0:1], min_val=0, max_val=MORE - 1) + (E - 1)
            with act.Fori(1, last_item) as i:
                item(i)
            item(last_item, last=True)
            act.wait_ge(scatter_done, last_item + 1)
            for t in range(TT):
                for half in range(2):
                    a.activation(gbuf[:, 0:512], psum[2 * t + half][:, :], ACT.Square,
                                 accum_out=small[:, 32 + 2 * t + half:33 + 2 * t + half]).then_inc(ssq4_ready, 1)
                    act.wait_ge(ssq4_ready, 2 * t + half + 1)
            act.wait_ge(var4, 1)
            a.activation(small[:, 40:42], small[:, 38:40], ACT.Sqrt).then_inc(root4, 1)

        @block.vector
        def _(dve):
            v = nc.vector
            chain = [0]

            def link(ins):
                chain[0] += 1
                ins.then_inc(dve_chain, 1)
                dve.wait_ge(dve_chain, chain[0])

            def job_of(kind, n):
                dve.wait_ge(job_done, number[kind, n] + 1)
                return bank_of(kind, n)

            def col(name, n=0, w=1):
                return vecT[:, COL[name] + n:COL[name] + n + w]

            dve.wait_ge(consts_ready, 2)
            pos = slotno[:, 0:ROW]
            for gi, w in enumerate((2, 4, 8, 16)):
                q = icnt[:, gi * ROW:(gi + 1) * ROW]
                t = m2[:, 0:ROW]
                link(v.tensor_scalar(t, pos, -1.0, float(ROW), ALU.mult, ALU.add))
                link(v.tensor_scalar(t, t, w / 2.0, None, ALU.min))
                link(v.tensor_scalar(q, pos, w / 2.0, None, ALU.min))
                link(v.tensor_tensor(q, q, t, ALU.add))
            v.reciprocal(icnt[:, :], icnt[:, :]).then_inc(consts_ready, 1)

            b = job_of("vec", 0)
            v.tensor_copy(vecT[:, :], b[:, 0:NVEC]).then_inc(read_dve, 1)
            dve.wait_ge(read_dve, 1)
            lam = col("lru_lambda", 0, 16)
            L = lambda n: lamw[:, 16 * n:16 * n + 16]
            link(v.tensor_scalar(L(2), lam, -1.0, None, ALU.mult))
            v.tensor_tensor(L(0), L(2), lam, ALU.max).then_inc(lam_abs, 1)
            dve.wait_ge(silu_th, 1)
            st = sT[:, :].rearrange("p (k s) -> p s k", s=2)
            cc = vecT[:, 0:16].rearrange("p (s k) -> p s k", s=2)
            th = small[:, 0:16].rearrange("p (s k) -> p s k", s=2)
            link(v.scalar_tensor_tensor(st, th, 1.0, cc, ALU.add, ALU.mult))
            v.tensor_scalar(sT[:, :], sT[:, :], 0.5, None, ALU.mult).then_inc(silu_ready, 1)
            dve.wait_ge(ssq_ready, 4)
            v.tensor_scalar(stat[:, 4:8], stat[:, 0:4], 1.0 / D, EPS, ALU.mult, ALU.add).then_inc(rstd_var, 1)
            dve.wait_ge(rstd_root, 1)
            link(v.reciprocal(stat[:, 8:12], stat[:, 8:12]))
            for t in range(4):
                v.tensor_scalar(xin[:, t, :], xin[:, t, :], stat[:, 8 + t:9 + t], None, ALU.mult).then_inc(tok_scaled, 1)
            dve.wait_ge(lam_exp, 1)
            link(v.tensor_scalar(L(3), L(1), 2.0, None, ALU.add))
            link(v.reciprocal(L(3), L(3)))
            link(v.tensor_tensor(L(1), L(1), L(3), ALU.mult))
            link(v.tensor_tensor(L(3), L(1), L(1), ALU.mult))
            link(v.tensor_scalar(L(0), L(3), 1.0 / 15, 1.0 / 13, ALU.mult, ALU.add))
            for n in (11, 9, 7, 5, 3, 1):
                link(v.tensor_tensor(L(0), L(0), L(3), ALU.mult))
                link(v.tensor_scalar(L(0), L(0), 1.0 / n, None, ALU.add))
            link(v.scalar_tensor_tensor(L(0), L(0), 2.0, L(1), ALU.mult, ALU.mult))
            link(v.tensor_scalar(L(2), L(2), 0.0, None, ALU.max))
            link(v.tensor_tensor(L(0), L(0), L(2), ALU.add))
            v.tensor_scalar(L(4), col("lru_ba", 0, 16), 0.5, None, ALU.mult)
            v.tensor_scalar(L(5), col("lru_bx", 0, 16), 0.5, None, ALU.mult)
            v.tensor_scalar(L(6), L(0), 2.0, None, ALU.mult)
            v.tensor_scalar(L(7), L(0), -4.0, None, ALU.mult).then_inc(lru_consts, 1)

            for c in range(8):
                b = job_of("mod", c)
                v.tensor_copy(modrow[:, c * CHUNK:(c + 1) * CHUNK], b[0:2, 0:CHUNK]).then_inc(read_dve, 1)
            b = job_of("mt", 0)
            bm = col("b_mod", 0, 16).rearrange("p (j s) -> p j s", s=1).broadcast_to([P, 16, 2])
            v.tensor_tensor(modT[:, :].rearrange("p (j s) -> p j s", s=2), b[:, 0:32].rearrange("p (j s) -> p j s", s=2),
                            bm, ALU.add).then_inc(read_dve, 1)
            dve.wait_ge(read_dve, read_at[number["mt", 0]][1])
            am = amod[:, :].rearrange("p (k s) -> p k s", s=2)
            gb = col("norm_pre_mix", 0, 8).rearrange("p (k s) -> p k s", s=1).broadcast_to([P, KT, 2])
            v.scalar_tensor_tensor(am, modT[:, 16:32].rearrange("p (k s) -> p k s", s=2), 1.0, gb,
                                   ALU.add, ALU.mult).then_inc(mod_ready, 1)
            b = job_of("b1", 0)
            v.tensor_copy(b1T[:, :], b[:, :]).then_inc(read_dve, 1)
            dve.wait_ge(mod_ready, 1)
            for k in range(1, KT, 2):
                b = job_of("xt", k)
                for s in range(2):
                    m = 1 - s
                    ins = v.tensor_scalar(uT[:, k, s * CTX:(s + 1) * CTX], b[:, s * CTX:(s + 1) * CTX],
                                          amod[:, 2 * k + m:2 * k + m + 1], modT[:, 2 * k + m:2 * k + m + 1],
                                          ALU.mult, ALU.add)
                ins.then_inc(read_dve, 1)
            dve.wait_ge(job_done, number["xt", KT - 1] + 1)
            for j in range(KT):
                dve.wait_ge(read_act, read_at[number["xr", j]][1])
                o = xc[:, j, :].rearrange("p (s t) -> p s t", s=2)
                link(v.tensor_scalar(o, xrp[:, j, :, 0:CTX], col("conv_w", j), col("conv_b", j), ALU.mult, ALU.add))
                for w in range(1, CONV):
                    ins = v.scalar_tensor_tensor(o, xrp[:, j, :, w:w + CTX], col("conv_w", w * KT + j), o,
                                                 ALU.mult, ALU.add)
                    if w < CONV - 1:
                        link(ins)
                ins.then_inc(conv_done, 1)
            for s in range(2 * HEADS):
                h, d = s // 2, s % 2
                dve.wait_ge(coef_ready, s + 1)
                xh = xc[:, 2 * h:2 * h + 2, :]
                v.scalar_tensor_tensor(amul, dec, 1.0, tnh, ALU.add, ALU.mult)
                v.scalar_tensor_tensor(rt, dec, 1.0, rt, ALU.add, ALU.mult)
                link(v.scalar_tensor_tensor(bb, thi, 1.0, xh, ALU.add, ALU.mult))
                v.tensor_scalar(amul, amul, -1.0, 1.0, ALU.mult, ALU.add)
                link(v.scalar_tensor_tensor(bb, bb, 0.5, rt, ALU.mult, ALU.mult))
                for j in range(2):
                    ca, cb = amul[:, j, 0:CTX], bb[:, j, 0:CTX]
                    if d:
                        ca, cb = ca[:, ::-1], cb[:, ::-1]
                    ins = v.tensor_tensor_scan(hs[:, j, 0:CTX], ca, cb, 0.0, ALU.mult, ALU.add)
                link(ins)
                for j in range(2):
                    ca, cb = amul[:, j, CTX:TOK], bb[:, j, CTX:TOK]
                    if d:
                        ca, cb = ca[:, ::-1], cb[:, ::-1]
                    o = hs[:, j, CTX:TOK] if d else hT[:, 2 * h + j, :]
                    ins = v.tensor_tensor_scan(o, ca, cb, hs[:, j, CTX - 1:CTX], ALU.mult, ALU.add)
                if d:
                    link(ins)
                    for j in range(2):
                        q = 2 * h + j
                        ins = v.tensor_tensor(hT[:, q, :], hT[:, q, :], hs[:, j, CTX:TOK][:, ::-1], ALU.add)
                ins.then_inc(lru_done, 1)
                dve.wait_ge(lru_done, s + 1)
            dve.wait_ge(gelu_ready, 1)
            v.scalar_tensor_tensor(gbuf[:, :], hbuf[:, :], 0.5 * 2, gbuf[:, :], ALU.mult, ALU.mult).then_inc(yrnn_ready, 1)
            for c in range(4):
                r = slice(c * 512, (c + 1) * 512)
                if c == 0:
                    dve.wait_ge(read_act, read_at[number["mp", 3]][1])
                b = job_of("rp", c)
                v.scalar_tensor_tensor(m1[:, r], m1[:, r], 1.0, b[:, :], ALU.add, ALU.mult).then_inc(read_dve, 1)
                b = job_of("pp", c)
                ins = v.scalar_tensor_tensor(m2[:, r], m2[:, r], 1.0, b[:, :], ALU.add, ALU.mult)
                ins.then_inc(read_dve, 1)
                dve.wait_ge(read_dve, read_at[number["pp", c]][1])
                v.tensor_tensor(bufB[:, 2048 + c * 512:2048 + (c + 1) * 512], m1[:, r], m2[:, r],
                                ALU.add).then_inc(merged_ready, 1)
            dve.wait_ge(brow_landed, 64)
            dve.wait_ge(nrow_landed, 48)
            for n in range(8):
                b = job_of("rs", n)
                r = rows[:, n // 2, (n % 2) * 512:(n % 2 + 1) * 512]
                v.tensor_tensor(r, r, b[:, :], ALU.add).then_inc(read_dve, 1)
            dve.wait_ge(read_dve, read_at[number["rs", 7]][1])
            v.tensor_tensor(rows[:, 0, :], rows[:, 0, :], nrow[:, 0, :], ALU.mult)
            v.scalar_tensor_tensor(rows[:, 1, :], rows[:, 1, :], 1.0, nrow[:, 1, :], ALU.add, ALU.mult)
            v.tensor_tensor(rows[:, 3, :], rows[:, 3, :], nrow[:, 2, :], ALU.mult).then_inc(rows_ready, 1)
            dve.wait_ge(rows_ready, 1)

            def make_lo(i, c):
                if c in DVE_LO:
                    raw_ap, _, _ = raw(c)
                    dve.wait_ge(hi_done, i * CPI + (c + 1))
                    v.tensor_tensor(wlo[c % SPLITS].rearrange("p k n -> p (k n)"), raw_ap,
                                    whi[c % SPLITS].rearrange("p k n -> p (k n)").bitcast(F32),
                                    ALU.subtract).then_inc(lo_dve, 1)

            dve.wait_ge(ssq2_ready, 8)
            link(v.tensor_reduce(stat[:, 12:14], small[:, 64:72].rearrange("p (t c) -> p t c", t=TT), AX.X, ALU.add))
            v.tensor_scalar(stat[:, 14:16], stat[:, 12:14], 1.0 / D, EPS, ALU.mult, ALU.add).then_inc(var2, 1)
            dve.wait_ge(root2, 1)
            link(v.reciprocal(stat[:, 18:20], stat[:, 16:18]))
            dve.wait_ge(xres_landed, 16)
            for t in range(TT):
                link(v.scalar_tensor_tensor(mlat[:, t, :], mlat[:, t, :], stat[:, 18 + t:19 + t], rows[:, 0, :],
                                            ALU.mult, ALU.mult))
                v.tensor_tensor(x1[:, t, :], x1[:, t, :], mlat[:, t, :], ALU.add).then_inc(x1_ready, 1)
            make_lo(0, 0)
            dve.wait_ge(ssq3_ready, TT)
            v.tensor_scalar(stat[:, 22:24], stat[:, 20:22], 1.0 / D, EPS, ALU.mult, ALU.add).then_inc(var3, 1)
            dve.wait_ge(root3, 1)
            link(v.reciprocal(stat[:, 26:28], stat[:, 24:26]))
            for t in range(TT):
                link(v.scalar_tensor_tensor(vtok[:, t, :], x1[:, t, :], stat[:, 26 + t:27 + t], rows[:, 1, :],
                                            ALU.mult, ALU.mult))
                v.tensor_tensor(vtok[:, t, :], vtok[:, t, :], rows[:, 2, :], ALU.add).then_inc(v_ready, 1)
            for n in (1, 3):
                b = job_of("vt", n)
                ins = v.tensor_copy(m2[:, n * 512:(n + 1) * 512], b[:, :])
                ins.then_inc(read_dve, 1)
            for c in range(1, AHEAD):
                make_lo(0, c)
            b = job_of("lg", 0)
            rbb = rb[:, :].rearrange("p (t e) -> p t e", t=1).broadcast_to([P, TT, E])
            ins = v.tensor_tensor(lg, b[:, 0:64].rearrange("p (t e) -> p t e", t=TT), rbb, ALU.add)
            ins.then_inc(read_dve, 1)
            dve.wait_ge(read_dve, read_at[number["lg", 0]][1])
            for t in range(TT):
                ins = v.max(mx[:, t, :], lg[:, t, :])
            link(ins)
            v.tensor_scalar(stat[:, 28:30], mx[:, :, 0], -1.0, None, ALU.mult).then_inc(neg_max, 1)
            for t in range(TT):
                ins = v.max_index(ixu[:, 8 * t:8 * t + 8], mx[:, t, :], lg[:, t, :])
            link(ins)
            link(v.tensor_copy(ixf, ixu[:, :].rearrange("p (t k) -> p t k", t=TT)))
            ib = ecol[:, 0:E].rearrange("p (k e) -> p k e", k=1).broadcast_to([P, TOPK, E])
            for t in range(TT):
                xb = ixf[:, t, 0:TOPK].rearrange("p (k e) -> p k e", e=1).broadcast_to([P, TOPK, E])
                ins = v.tensor_tensor(oh[:, t], ib, xb, ALU.is_equal)
            link(ins)
            v.tensor_reduce(mask, oh.rearrange("p t k e -> p t e k"), AX.X, ALU.add).then_inc(mask_ready, 1)
            dve.wait_ge(exps_ready, TT)
            link(v.reciprocal(small[:, 48:50], stat[:, 30:32]))
            for t in range(TT):
                ins = v.tensor_scalar(ew[:, t, :], ew[:, t, :], small[:, 48 + t:49 + t], None, ALU.mult)
            link(ins)
            for t in range(TT):
                wb = ew[:, t, :].rearrange("p (k e) -> p k e", e=1).broadcast_to([P, TOPK, E])
                ins = v.tensor_tensor(ohw[:, t], oh[:, t], wb, ALU.mult)
            link(ins)
            v.tensor_reduce(comb_v, ohw.rearrange("p t k e -> p t e k"), AX.X, ALU.add).then_inc(comb_ready, 1)
            b = job_of("rk", 0)
            dve.wait_ge(mask_ready, 1)
            link(v.scalar_tensor_tensor(rank[:, :], b[:, 0:64], 1.0, mask.rearrange("p t e -> p (t e)"), ALU.add, ALU.mult))
            link(v.tensor_scalar(rank[:, :], rank[:, :], -1.0, None, ALU.add))
            v.tensor_copy(cnt, b[0:1, 64:96]).then_inc(read_dve, 1)
            dve.wait_ge(comb_ready, 1)

            def one_hot(e, r):
                for t in range(TT):
                    ins = v.tensor_scalar(sel[:, t, :], slotno[:, ds(r * 128, SLOTS)], rank[:, ds(e + t * E, 1)], None,
                                          ALU.is_equal)
                ins.then_inc(sel_ready, 1)

            def weighted(e, r):
                for t in range(TT):
                    ins = v.tensor_scalar(selw[:, t, :], slotno[:, ds(r * 128, 128)], rank[:, ds(e + t * E, 1)],
                                          comb[:, ds(e + t * E, 1)], ALU.is_equal, ALU.mult)
                ins.then_inc(selw_ready, 1)

            one_hot(0, 0)
            weighted(0, 0)

            def take_tokens(n):
                dve.wait_ge(xhi_ready, n)
                v.tensor_tensor(xhl[:, :, 1, :], psum[7][:, :].rearrange("p (k c) -> p k c", k=KT),
                                xhl[:, :, 0, :].bitcast(F32), ALU.subtract).then_inc(xlo_ready, 1)

            b = job_of("ct", 0)
            v.tensor_copy(combT, b[0:E, 0:SEQ]).then_inc(read_dve, 1)
            take_tokens(1)
            for r in range(3):
                ins = v.tensor_scalar(ovr[:, r, :], cnt, float(SLOTS * (r + 1)), None, ALU.is_gt)
            link(ins)
            link(v.tensor_reduce(ovs, ovr.rearrange("p r e -> p e r"), AX.X, ALU.add))
            link(v.tensor_tensor_scan(inc, ones[0:1, 0:E], ovs, 0.0, ALU.mult, ALU.add))
            link(v.tensor_copy(more[0:1, :], inc[:, E - 1:E]))
            link(v.tensor_tensor(inc, inc, ovs, ALU.subtract))
            for r in range(3):
                ins = v.scalar_tensor_tensor(posr[:, r, :], inc, float(r + 1), ovr[:, r, :], ALU.add, ALU.mult)
            link(ins)
            pb = posr.rearrange("p r e -> p (r e)").rearrange("p (j q) -> p j q", j=1).broadcast_to([1, MORE, 96])
            jb = jcol[0:1, :].rearrange("p (j q) -> p j q", q=1).broadcast_to([1, MORE, 96])
            for vals, tab in ((ecol, tabE), (rcol, tabR)):
                vb = vals[0:1, :].rearrange("p (j q) -> p j q", j=1).broadcast_to([1, MORE, 96])
                link(v.tensor_tensor(ojh, pb, jb, ALU.is_equal))
                link(v.tensor_tensor(ojh, ojh, vb, ALU.mult))
                link(v.tensor_reduce(tabf[:, 0:MORE], ojh, AX.X, ALU.add))
                link(v.tensor_copy(tab[:, E:ITEMS], tabf[:, 0:MORE]))
            v.tensor_copy(tabE[:, 0:E], ecol[0:1, 0:E])
            v.memset(tabR[:, 0:E], 0).then_inc(items_ready, 1)
            dve.wait_ge(items_ready, 1)
            last_item = dve.value_load(more[0:1, 0:1], min_val=0, max_val=MORE - 1) + (E - 1)

            base = chain[0]
            CH = 6

            def item(i, last=False):
                def step(ins, n):
                    ins.then_inc(dve_chain, 1)
                    dve.wait_ge(dve_chain, i * CH + (base + n))

                def ahead(c):
                    n = c + AHEAD
                    if n < CPI:
                        make_lo(i, n)
                    elif not last:
                        make_lo(i + 1, n - CPI)

                def biased(p, half, dst):
                    dve.wait_ge(fold_done, i * 4 + (2 * p + half + 1))
                    bias = b1T[:, ds(e0 * 16 + (8 * half + 4 * p), 4)].rearrange("p (f c) -> p f c", c=1).broadcast_to(
                        [P, 4, SLOTS])
                    step(v.tensor_tensor(dst.rearrange("p (f c) -> p f c", f=4),
                                         psum[6][:, half * 256:half * 256 + 256].rearrange("p (f c) -> p f c", f=4),
                                         bias, ALU.add), 3 * p + half + 1)

                def gate(p):
                    biased(p, 0, glu)
                    v.tensor_scalar(glu, glu, LIMIT, None, ALU.min).then_inc(glu_ready, 1)

                def linear(p):
                    dve.wait_ge(glu_ready, i * 2 + (p + 1))
                    biased(p, 1, lin)
                    dve.wait_ge(sig_ready, i * 2 + (p + 1))
                    v.tensor_scalar(lin, lin, LIMIT, -LIMIT, ALU.min, ALU.max)
                    step(v.tensor_tensor(sg, glu, sg, ALU.mult), 3 * p + 3)
                    v.scalar_tensor_tensor(actf, lin, 1.0, sg, ALU.add, ALU.mult).then_inc(act_ready, 1)

                def act_lo(p):
                    dve.wait_ge(ahi_ready, i * 2 + (p + 1))
                    v.tensor_tensor(ahl[:, 4 * p:4 * p + 4, 1, :], actf.rearrange("p (f c) -> p f c", f=4),
                                    ahl[:, 4 * p:4 * p + 4, 0, :].bitcast(F32), ALU.subtract).then_inc(alo_ready, 1)

                e0 = dve.value_load(tabE[0:1, ds(i, 1)], min_val=0, max_val=E - 1)
                if not last:
                    e1 = dve.value_load(tabE[0:1, ds(i + 1, 1)], min_val=0, max_val=E - 1)
                    r1 = dve.value_load(tabR[0:1, ds(i + 1, 1)], min_val=0, max_val=3)
                ahead(0)
                if not last:
                    one_hot(e1, r1)
                ahead(1)
                ahead(2)
                ahead(3)
                gate(0)
                linear(0)
                ahead(4)
                act_lo(0)
                if not last:
                    dve.wait_ge(gt_done, i + 1)
                    weighted(e1, r1)
                ahead(5)
                ahead(6)
                gate(1)
                linear(1)
                ahead(7)
                act_lo(1)
                ahead(8)
                if not last:
                    take_tokens(i + 2)
                ahead(9)
                ahead(10)
                ahead(11)

            item(0)
            with dve.Fori(1, last_item) as i:
                item(i)
            item(last_item, last=True)
            dve.wait_ge(ssq4_ready, 4)
            fs = small[:, 32:36].rearrange("p (t h) -> p t h", t=TT)
            tail = [0]

            def then(ins):
                tail[0] += 1
                ins.then_inc(tail_chain, 1)
                dve.wait_ge(tail_chain, tail[0])

            then(v.tensor_tensor(small[:, 36:38], fs[:, :, 0], fs[:, :, 1], ALU.add))
            v.tensor_scalar(small[:, 38:40], small[:, 36:38], 1.0 / D, EPS, ALU.mult, ALU.add).then_inc(var4, 1)
            dve.wait_ge(root4, 1)
            then(v.reciprocal(small[:, 42:44], small[:, 40:42]))
            for t in range(TT):
                for half in range(2):
                    r = slice(half * 512, (half + 1) * 512)
                    ins = v.scalar_tensor_tensor(m2[:, r], psum[2 * t + half][:, :], small[:, 42 + t:43 + t],
                                                 rows[:, 3, r], ALU.mult, ALU.mult)
                then(ins)
                v.tensor_tensor(x1[:, t, :], x1[:, t, :], m2[:, 0:D], ALU.add).then_inc(out_ready, 1)
                dve.wait_ge(out_ready, t + 1)


_INS = ["x", "c", "ctx", "c_ctx", "w_mod", "b_mod", "norm_pre_mix", "norm_post_mix", "norm_pre_ffn",
        "norm_post_ffn", "w_in", "conv_w", "conv_b", "lru_wa", "lru_ba", "lru_wx", "lru_bx", "lru_lambda",
        "pool_w", "pool_scale", "w_rnn_proj", "w_pool_proj", "w_out", "router_w", "router_b",
        "exp_w1", "exp_b1", "exp_w2", "exp_b2"]


def kernel(**inputs):
    import concourse.bacc as bacc
    from concourse.bass_utils import run_bass_kernel_spmd

    nc = bacc.Bacc("TRN2", target_bir_lowering=False, num_devices=1)
    arrays, aps = {}, {}
    for name in _INS:
        a = np.ascontiguousarray(inputs[name])
        arrays[f"in_{name}"] = a
        aps[name] = nc.dram_tensor(f"in_{name}", a.shape, mybir.dt.from_np(a.dtype), kind="ExternalInput").ap()
    out = nc.dram_tensor("out", (1, SEQ, D), F32, kind="ExternalOutput").ap()
    build(nc, aps, out)
    r = run_bass_kernel_spmd(nc, [arrays], core_ids=[0])
    return r.results[0]["out"]
```

```python
from contextlib import ExitStack

import numpy as np
import concourse.bass as bass
from concourse import mybir

F32 = mybir.dt.float32
F32R = mybir.dt.float32r
I32 = mybir.dt.int32
U32 = mybir.dt.uint32
ALU = mybir.AluOpType
ACT = mybir.ActivationFunctionType
AX = mybir.AxisListType
ds = bass.ds

P = 128
D = 1024
KT = D // P
SEQ = 256
CTX = 256
TOK = CTX + SEQ
TT = SEQ // P
HEADS = 4
ROW = 64
ROWS = SEQ // ROW
PAD = 8
PROW = ROW + 2 * PAD
CONV = 4
E = 32
TOPK = 4
SLOTS = 64
MORE = 16
ITEMS = E + MORE
EPS = 1e-6
LIMIT = 7.0
ALPHA = 1.702
CHUNK = 256
CW = KT * CHUNK
RING = 4
BANK = 512
CPI = 12
HALF = 512
HIS = 4
AHEAD = HIS - 1
BLOCK_COL = [0, D, HALF, D + HALF]
DVE_COLS = 3 * HALF
ARENA = 12 * CW
ARENA_CHUNKS = ARENA // CW - HIS

ROWS1 = [("c", 8), ("c_ctx", 8), ("norm_pre_mix", 8), ("norm_post_mix", 8), ("norm_pre_ffn", 8),
         ("norm_post_ffn", 8), ("b_mod", 48), ("conv_w", 32)]
ROWS2 = [("conv_b", 8), ("lru_ba", 16), ("lru_bx", 16), ("lru_lambda", 16), ("pool_scale", 8)]
COL = {}
for _rows, _base in ((ROWS1, 0), (ROWS2, P)):
    _at = _base
    for _name, _n in _rows:
        COL[_name] = _at
        _at += _n
NVEC = P + 64


def front_plan():
    plan = [("vec", 0, "V")]
    plan += [("mod", c, "V") for c in range(8)]
    plan += [("mt", 0, "V"), ("b1", 0, "V")]
    plan += [("xt", k, "AV"[k % 2]) for k in range(KT)]
    plan += [("xr", j, "A") for j in range(KT)]
    for s in range(2 * HEADS):
        plan += [("lru", s, None), ("xp", s, "A") if s < 4 else ("gg", s - 4, "A")]
    plan += [("mr", c, "A") for c in range(4)] + [("mp", c, "A") for c in range(4)]
    plan += [("pw", g, "A") for g in range(4)]
    for c in range(4):
        plan += [("rp", c, "V"), ("pp", c, "V")]
    plan += [("rs", n, "V") for n in range(8)]
    plan += [("wo", c, "A") for c in range(4)]
    plan += [("vt", n, "AV"[n % 2]) for n in range(4)]
    plan += [("lg", 0, "V"), ("rk", 0, "V"), ("ct", 0, "V")]
    return plan


def build(nc, I, out):
    ctx = ExitStack()
    with ctx:
        def sb(name, shape, dt=F32):
            return ctx.enter_context(nc.sbuf_tensor(name, shape, dt))

        def sem(name):
            return ctx.enter_context(nc.semaphore(name))

        arena_at = -(-nc.sbuf_base // 32) * 32
        arena = sb("arena", [P, ARENA])
        ring_at = -(-nc.sbuf_base // 32) * 32
        ring = sb("ring", [P, RING * CW])
        bufA = sb("bufA", [P, 4096])
        bufB_at = -(-nc.sbuf_base // 32) * 32
        bufB = sb("bufB", [P, 4096])
        gbuf = sb("gbuf", [P, 2048])
        hbuf = sb("hbuf", [P, 2048])
        m1 = sb("m1", [P, 2048])
        m2 = sb("m2", [P, 2048])
        psum = [ctx.enter_context(nc.psum_tensor(f"bank{b}", [P, BANK], F32)) for b in range(8)]

        ident = sb("ident", [P, P])
        ones = sb("ones", [P, P])
        upper = sb("upper", [P, P])
        iotaI = sb("iotaI", [P, 512], I32)
        slotno = sb("slotno", [P, 512])
        ecol = sb("ecol", [P, 96])
        rcol = sb("rcol", [P, 96])
        jcol = sb("jcol", [P, 1])
        icnt = sb("icnt", [P, 4 * ROW])
        vstage = sb("vstage", [P, 2 * P])
        vecT = sb("vecT", [P, NVEC])
        modT = sb("modT", [P, 32])
        sT = sb("sT", [P, 2 * KT])
        small = sb("small", [P, 160])
        lamw = sb("lamw", [P, 8 * 16])
        amod = sb("amod", [P, 2 * KT])
        folder = sb("folder", [P, SLOTS])
        stat = sb("stat", [P, 32])
        b1T = sb("b1T", [P, 512])
        rw = sb("rw", [P, KT * E])
        rb = sb("rb", [P, E])
        tabE = sb("tabE", [1, ITEMS], I32)
        tabR = sb("tabR", [1, ITEMS], I32)
        more = sb("more", [1, 1], I32)
        rank = sb("rank", [P, TT * E])
        comb = sb("comb", [P, TT * E])

        xin = bufA[:, :].rearrange("p (t d) -> p t d", t=4)
        xc = bufA[:, :].rearrange("p (j t) -> p j t", j=KT)
        rows = bufA[:, :].rearrange("p (r d) -> p r d", r=4)
        uT = bufB[:, :].rearrange("p (j t) -> p j t", j=KT)
        ypT = bufB[:, 0:2048].rearrange("p (j t) -> p j t", j=KT)
        mgT = bufB[:, 2048:4096].rearrange("p (j t) -> p j t", j=KT)
        gT = gbuf[:, :].rearrange("p (j t) -> p j t", j=KT)
        mlat = gbuf[:, :].rearrange("p (t d) -> p t d", t=TT)
        hT = hbuf[:, :].rearrange("p (j t) -> p j t", j=KT)
        x1 = hbuf[:, :].rearrange("p (t d) -> p t d", t=TT)
        vtok = m1[:, :].rearrange("p (t d) -> p t d", t=TT)
        vT = m2[:, :].rearrange("p (j t) -> p j t", j=KT)
        gchunk = [arena[:, n * CW:(n + 1) * CW].rearrange("p (k n) -> p k n", k=KT) for n in range(2)]
        modrow = m1[0:2, :]

        def colsum(q):
            o = 2 * CW + q * CHUNK if q < 8 else 10240 + (q - 8) * CHUNK
            return arena[:, o:o + CHUNK]

        o = 6144
        GP = 2 * ROWS * PROW
        xpp = arena[:, o:o + 4 * GP].rearrange("p (g r q) -> p g r q", g=4, q=PROW)
        winA = arena[:, o + 4 * GP:o + 5 * GP].rearrange("p (r q) -> p r q", q=PROW)
        winB = arena[:, o + 5 * GP:o + 6 * GP].rearrange("p (r q) -> p r q", q=PROW)
        CP = CTX + CONV - 1
        o = 10240
        xrp = arena[:, o:o + KT * 2 * CP].rearrange("p (j s t) -> p j s t", j=KT, s=2)

        def tmp(n):
            a = 16384 + n * 1024
            return arena[:, a:a + 1024].rearrange("p (j t) -> p j t", j=2)
        thr, thi, tnh, dec, rt, amul, bb, hs = (tmp(n) for n in range(8))
        nrow = arena[:, 21504:24576].rearrange("p (r d) -> p r d", r=3)
        def alias(name, n, at):
            return nc.alloc_sbuf_tensor_at(name, [P, n], F32R, offset=at)

        def as_chunk(t):
            return t[:, :].rearrange("p (k n) -> p k n", k=4)
        whi = [as_chunk(alias(f"whi{q}", CW, arena_at + 4 * CW * q)) for q in range(HIS)]
        raw, wlo = [], []
        for c in range(CPI):
            if c < ARENA_CHUNKS:
                o, buf, at = (HIS + c) * CW, arena, arena_at
            else:
                o, buf, at = (c - ARENA_CHUNKS) * CW, ring, ring_at
            raw.append(buf[:, o:o + CW].rearrange("p (k n) -> p k n", k=4))
            wlo.append(as_chunk(alias(f"wlo{c}", CW, at + 4 * o)))
        RB = bufB
        lg = RB[:, 0:64].rearrange("p (t e) -> p t e", t=TT)
        mx = RB[:, 64:80].rearrange("p (t k) -> p t k", t=TT)
        ixf = RB[:, 80:96].rearrange("p (t k) -> p t k", t=TT)
        ew = RB[:, 96:104].rearrange("p (t k) -> p t k", t=TT)
        mask = RB[:, 128:192].rearrange("p (t e) -> p t e", t=TT)
        oh = RB[:, 192:448].rearrange("p (t k e) -> p t k e", t=TT, k=TOPK)
        ohw = RB[:, 448:704].rearrange("p (t k e) -> p t k e", t=TT, k=TOPK)
        cnt = RB[0:MORE, 704:736]
        ovr = RB[0:MORE, 736:832].rearrange("p (r e) -> p r e", r=3)
        ovs = RB[0:MORE, 832:864]
        inc = RB[0:MORE, 864:896]
        combT = RB[0:E, 896:1152]
        posr = RB[0:MORE, 1152:1248].rearrange("p (r e) -> p r e", r=3)
        exc = RB[0:MORE, 1248:1280]
        look = RB[0:MORE, 192:384].rearrange("p (q n) -> p q n", q=2)
        tabf = RB[0:MORE, 384:386]
        ixu = sb("ixu", [P, 16], U32)
        b2s = gbuf[0:E, 0:1024]
        b1stage = m2[:, 1024:1536].rearrange("p (n q) -> p n q", n=4)
        rank_v = rank[:, :].rearrange("p (t e) -> p t e", t=TT)
        comb_v = comb[:, :].rearrange("p (t e) -> p t e", t=TT)
        sel = bufB[:, 1408:1536].rearrange("p (t c) -> p t c", t=TT)
        selw = bufB[:, 1536:1792].rearrange("p (t c) -> p t c", t=TT)
        gt = bufB[:, 1792:2048]
        xhl = alias("xhl", 1024, bufB_at + 4 * 2048)[:, :].rearrange("p (k q c) -> p k q c", k=KT, q=2)
        ahl = alias("ahl", 1024, bufB_at + 4 * 3072)[:, :].rearrange("p (k q c) -> p k q c", k=KT, q=2)
        zS = [gbuf[:, 1024 + q * 512:1536 + q * 512] for q in range(2)]
        yS = m2[:, 0:1024]
        mout = m2[:, :].rearrange("p (t d) -> p t d", t=TT)
        glu, lin, sg, actf = (m2[:, 1024 + q * 256:1280 + q * 256] for q in range(4))

        ring_landed = [sem(f"ring_landed{r}") for r in range(RING)]
        expert_landed = [sem(f"expert_landed{c}") for c in range(CPI)]
        vecs_landed, tokens_landed, late_landed = sem("vecs_landed"), sem("tokens_landed"), sem("late_landed")
        xres_landed = sem("xres_landed")
        hi_done, lo_dve, lo_pool = sem("hi_done"), sem("lo_dve"), sem("lo_pool")
        w_used = sem("w_used")
        gmod_landed = [sem(f"gmod_landed{n}") for n in range(2)]
        sums_ready, brow_landed, nrow_landed, rows_ready = sem("sums_ready"), sem("brow_landed"), sem("nrow_landed"), sem("rows_ready")
        z_ready, fold_done, xlo_ready, ahi_ready, alo_ready = (
            sem(n) for n in ("z_ready", "fold_done", "xlo_ready", "ahi_ready", "alo_ready"))
        out_written = sem("out_written")
        consts_ready, pads_ready = sem("consts_ready"), sem("pads_ready")
        job_done = sem("job_done")
        read_act, read_dve = sem("read_act"), sem("read_dve")
        ssq_ready, rstd_var, rstd_root, tok_scaled = sem("ssq_ready"), sem("rstd_var"), sem("rstd_root"), sem("tok_scaled")
        silu_th, silu_ready = sem("silu_th"), sem("silu_ready")
        lam_abs, lam_exp, lru_consts = sem("lam_abs"), sem("lam_exp"), sem("lru_consts")
        mod_ready = sem("mod_ready")
        conv_done = sem("conv_done")
        gates_done, gates_read, coef_ready, lru_done = sem("gates_done"), sem("gates_read"), sem("coef_ready"), sem("lru_done")
        gelu_ready, yrnn_ready, pool_ready = sem("gelu_ready"), sem("yrnn_ready"), sem("pool_ready")
        merged_ready = sem("merged_ready")
        ssq2_ready, var2, root2, x1_ready, v_ready, ssq3_ready, var3, root3 = (
            sem(n) for n in ("ssq2_ready", "var2", "root2", "x1_ready", "v_ready", "ssq3_ready", "var3", "root3"))
        neg_max, exps_ready, mask_ready, comb_ready = (
            sem(n) for n in ("neg_max", "exps_ready", "mask_ready", "comb_ready"))
        table_ready, table_done, items_ready = sem("table_ready"), sem("table_done"), sem("items_ready")
        sel_ready, selw_ready, gather_done, xhi_ready = sem("sel_ready"), sem("selw_ready"), sem("gather_done"), sem("xhi_ready")
        glu_ready, sig_ready, act_ready = sem("glu_ready"), sem("sig_ready"), sem("act_ready")
        gt_done, gt_ready, y_ready, scatter_done = (
            sem(n) for n in ("gt_done", "gt_ready", "y_ready", "scatter_done"))
        ssq4_ready, var4, root4, out_ready = sem("ssq4_ready"), sem("var4"), sem("root4"), sem("out_ready")
        act_warm = sem("act_warm")
        act_chain, dve_chain, pool_chain, tail_chain = sem("act_chain"), sem("dve_chain"), sem("pool_chain"), sem("tail_chain")

        plan = front_plan()
        number, reads = {}, {"A": 0, "V": 0}
        read_at = []
        for kind, n, reader in plan:
            if kind == "lru":
                continue
            number[kind, n] = len(read_at)
            reads[reader] += 1
            read_at.append((reader, reads[reader]))
        JOBS = len(read_at)

        def bank_of(kind, n):
            return psum[4 + number[kind, n] % 4]

        def cols(w, c):
            return w[:, c * CHUNK:(c + 1) * CHUNK].rearrange("(k p) n -> p k n", p=P)

        w_in, w_mod = I["w_in"][0], I["w_mod"][0]
        ROW_GROUP = [2, 4, 3, 5]
        chunks, chunk_no = [], {}
        for kind, n, _ in plan:
            c = None
            if kind == "mod":
                c = [(cols(w_mod, n), 0)]
            elif kind == "xr" and n % 2 == 0:
                c = [(cols(w_in, n // 2), 0)]
            elif kind == "lru":
                h, d = n // 2, n % 2
                c = [(I[w][0, d, h].rearrange("(k p) n -> p k n", p=P), q * 512)
                     for q, w in enumerate(("lru_wa", "lru_wx"))]
            elif kind in ("gg", "xp", "mr", "mp"):
                c = [(cols(w_in, {"gg": 4, "xp": 8, "mr": 12, "mp": 16}[kind] + n), 0)]
            elif kind == "pw" and n == 0:
                c = [(I["pool_w"][0].rearrange("g (k p) n -> p g k n", p=P), 0)]
            elif kind in ("rp", "pp", "wo"):
                c = [(cols(I[{"rp": "w_rnn_proj", "pp": "w_pool_proj", "wo": "w_out"}[kind]][0], n), 0)]
            if c:
                chunk_no[kind, n] = len(chunks)
                chunks.append(c)
        landed, per = [], [0] * RING
        for n, c in enumerate(chunks):
            per[n % RING] += 16 * len(c)
            landed.append(per[n % RING])

        def chunk_of(kind, n):
            r = chunk_no[kind, n] % RING
            return ring[:, r * CW:(r + 1) * CW]

        def chunk_used(n):
            kind, m = next(key for key, c in chunk_no.items() if c == n)
            if kind == "lru":
                return gates_done, m + 1
            if kind in ("xr", "pw"):
                m += {"xr": 1, "pw": 3}[kind]
            return job_done, number[kind, m] + 1

        NF = len(chunks)

        def lo_wait(eng, i, c):
            eng.wait_ge(lo_dve, i * CPI + (c + 1))
            eng.wait_ge(lo_pool, i * CPI + (c + 1))

        def block_of(c):
            return (c // 2, c % 2) if c < 8 else (4 + c % 2, (c - 8) // 2)

        def expert_src(e, c):
            b, q = block_of(c)
            w, col = (I["exp_w1"], BLOCK_COL[b]) if b < 4 else (I["exp_w2"], (b - 4) * HALF)
            return w[0, ds(e, 1), q * 512:(q + 1) * 512, col:col + HALF].rearrange("a (k p) n -> p (a k) n", p=P)

        def flat(chunk):
            return chunk.rearrange("p k n -> p (k n)")

        def load_vectors(eng, names):
            for name, n in names:
                src = I[name]
                while len(src.shape) > 1:
                    src = src.rearrange({2: "a b -> (a b)", 3: "a b c -> (a b c)"}[len(src.shape)])
                src = src.rearrange("(r q) -> r q", q=P)
                c = COL[name]
                o = c // P * P
                eng.dma_start(vstage[c - o:c - o + n, o:o + P], src).then_inc(vecs_landed, 16)

        def xrows(src):
            return src.broadcast_to([P, src.shape[-1]])

        block = ctx.enter_context(nc.Block())

        @block.sync
        def _(sp):
            def load_expert(e, c):
                sp.dma_start(raw[c], expert_src(e, c)).then_inc(expert_landed[c], 16)

            load_vectors(sp, (ROWS1 + ROWS2)[0::2])
            for n, parts in enumerate(chunks):
                if n >= RING:
                    sp.wait_ge(*chunk_used(n - RING))
                for src, o in parts:
                    r = (n % RING) * CW + o
                    w = int(np.prod(src.shape)) // P
                    dst = ring[:, r:r + w]
                    if len(src.shape) == 4:
                        dst = dst.rearrange("p (g k n) -> p g k n", g=src.shape[1], k=src.shape[2])
                    else:
                        dst = dst.rearrange("p (k n) -> p k n", k=src.shape[1])
                    sp.dma_start(dst, src).then_inc(ring_landed[n % RING], 16)
                if n == chunk_no["mp", 0]:
                    sp.wait_ge(lru_done, 2 * HEADS)
                    for r, g in enumerate(ROW_GROUP):
                        sp.dma_start(rows[:, r, :], xrows(I["b_mod"][0:1, g * D:(g + 1) * D])).then_inc(brow_landed, 16)
                    for r, name in enumerate(("norm_post_mix", "norm_pre_ffn", "norm_post_ffn")):
                        sp.dma_start(nrow[:, r, :], xrows(I[name])).then_inc(nrow_landed, 16)
                if n == chunk_no["rp", 0]:
                    sp.wait_ge(yrnn_ready, 1)
                    sp.dma_start(x1, I["x"][0].rearrange("(t p) d -> p t d", p=P)).then_inc(xres_landed, 16)
            for c in range(CPI):
                if c == 0:
                    sp.wait_ge(rows_ready, 1)
                if c == ARENA_CHUNKS:
                    sp.wait_ge(*chunk_used(NF - 1))
                load_expert(0, c)
            sp.wait_ge(items_ready, 1)
            last_item = sp.value_load(more[0:1, 0:1], min_val=0, max_val=MORE - 1) + (E - 1)
            with sp.Fori(1, last_item + 1) as i:
                e = sp.value_load(tabE[0:1, ds(i, 1)], min_val=0, max_val=E - 1)
                for c in range(CPI):
                    sp.wait_ge(w_used, (i - 1) * CPI + (c + 1))
                    load_expert(e, c)
            for t in range(TT):
                sp.wait_ge(out_ready, t + 1)
                sp.dma_start(out[0, t * P:(t + 1) * P, :], x1[:, t, :]).then_inc(out_written, 16)
            sp.wait_ge(out_written, 16 * TT)

        @block.gpsimd
        def _(pool):
            g = nc.gpsimd
            chain = [0]

            def link(ins):
                chain[0] += 1
                ins.then_inc(pool_chain, 1)
                pool.wait_ge(pool_chain, chain[0])

            g.memset(ident[:, :], 0.0)
            g.memset(upper[:, :], 1.0)
            link(g.memset(ones[:, :], 1.0))
            g.affine_select(out=ident[:, :], in_=ident[:, :], compare_op=ALU.not_equal, fill=1.0, base=0,
                            pattern=[[-1, P]], channel_multiplier=1)
            g.affine_select(out=upper[:, :], in_=upper[:, :], compare_op=ALU.is_gt, fill=0.0, base=0,
                            pattern=[[1, P]], channel_multiplier=-1).then_inc(consts_ready, 1)
            pool.dma_start(xin[:, 0:2, :], I["ctx"][0].rearrange("(t p) d -> p t d", p=P)).then_inc(tokens_landed, 16)
            pool.dma_start(xin[:, 2:4, :], I["x"][0].rearrange("(t p) d -> p t d", p=P)).then_inc(tokens_landed, 16)
            pool.wait_ge(consts_ready, 1)
            g.tensor_tensor(folder[:, :], ident[:, 0:SLOTS], ident[:, SLOTS:P], ALU.add)
            g.memset(xrp[:, :, :, 0:2], 0.0)
            g.memset(xrp[:, :, :, CP - 1:CP], 0.0)
            xz = xpp[:, :, :, :].rearrange("p g r q -> p (g r) q")
            g.memset(xz[:, :, 0:PAD], 0.0)
            g.memset(xz[:, :, PAD + ROW:PROW], 0.0).then_inc(pads_ready, 1)
            link(g.iota(iotaI[:, :], pattern=[[64, 4], [0, 2], [1, 64]], base=0, channel_multiplier=0))
            link(g.tensor_copy(slotno[:, :], iotaI[:, :]))
            link(g.iota(iotaI[:, 0:96], pattern=[[0, 3], [1, 32]], base=0, channel_multiplier=0))
            link(g.tensor_copy(ecol[:, :], iotaI[:, 0:96]))
            link(g.iota(iotaI[:, 0:96], pattern=[[1, 3], [0, 32]], base=1, channel_multiplier=0))
            link(g.tensor_copy(rcol[:, :], iotaI[:, 0:96]))
            link(g.iota(iotaI[:, 0:1], pattern=[[0, 1]], base=1, channel_multiplier=1))
            g.tensor_copy(jcol[:, :], iotaI[:, 0:1]).then_inc(consts_ready, 1)

            def gmod_load(q):
                c = ROW_GROUP[q // 4] * 4 + q % 4
                pool.dma_start(gchunk[q % 2], cols(w_mod, c)).then_inc(gmod_landed[q % 2], 16)

            def gmod_sum(q):
                w = gchunk[q % 2]
                pool.wait_ge(gmod_landed[q % 2], 16 * (q // 2 + 1))
                sb_ = sT[:, :].rearrange("p (k s) -> p k s", s=2)[:, :, 0:1].broadcast_to([P, KT, CHUNK])
                link(g.tensor_tensor(w, w, sb_, ALU.mult))
                link(g.tensor_tensor(w[:, 0:4], w[:, 0:4], w[:, 4:8], ALU.add))
                link(g.tensor_tensor(w[:, 0:2], w[:, 0:2], w[:, 2:4], ALU.add))
                g.tensor_tensor(colsum(q), w[:, 0], w[:, 1], ALU.add).then_inc(sums_ready, 1)
                pool.wait_ge(sums_ready, q + 1)
                if q + 2 < 16:
                    gmod_load(q + 2)

            gmod_load(0)
            gmod_load(1)
            pool.wait_ge(silu_ready, 1)
            for q in range(8):
                gmod_sum(q)
            for gi in range(4):
                pool.wait_ge(read_act, read_at[number["xp", gi]][1])
                x = xpp[:, gi]
                a, b = winA, winB
                link(g.tensor_tensor(a[:, :, 1:80], x[:, :, 0:79], x[:, :, 1:80], ALU.add))
                if gi >= 1:
                    link(g.tensor_tensor(b[:, :, 2:79], a[:, :, 1:78], a[:, :, 3:80], ALU.add))
                    a, b = b, a
                if gi >= 2:
                    link(g.tensor_tensor(b[:, :, 4:77], a[:, :, 2:75], a[:, :, 6:79], ALU.add))
                    a, b = b, a
                if gi >= 3:
                    link(g.tensor_tensor(b[:, :, 8:72], a[:, :, 4:68], a[:, :, 12:76], ALU.add))
                    a, b = b, a
                if gi == 0:
                    pool.wait_ge(consts_ready, 3)
                inv = icnt[:, gi * ROW:(gi + 1) * ROW].rearrange("p (a q) -> p a q", a=1).broadcast_to(
                    [P, 2 * ROWS, ROW])
                xs = x[:, :, PAD:PAD + ROW]
                link(g.tensor_tensor(a[:, :, 8:72], a[:, :, 8:72], inv, ALU.mult))
                g.tensor_tensor(xs, a[:, :, 8:72], xs, ALU.subtract).then_inc(pool_ready, 1)
                pool.wait_ge(pool_ready, gi + 1)
            pool.wait_ge(conv_done, KT)
            for q in range(8, 16):
                gmod_sum(q)

            def make_lo(i, c):
                pool.wait_ge(hi_done, i * CPI + (c + 1))
                g.tensor_tensor(flat(wlo[c])[:, DVE_COLS:], flat(raw[c])[:, DVE_COLS:],
                                flat(whi[c % HIS])[:, DVE_COLS:].bitcast(F32), ALU.subtract).then_inc(lo_pool, 1)

            for c in range(CPI):
                make_lo(0, c)
            pool.wait_ge(items_ready, 1)
            last_item = pool.value_load(more[0:1, 0:1], min_val=0, max_val=MORE - 1) + (E - 1)
            with pool.Fori(1, last_item + 1) as i:
                for c in range(CPI):
                    make_lo(i, c)

        @block.tensor
        def _(pe):
            mm = nc.tensor.matmul
            job = [0]

            def start_job():
                m = job[0]
                if m >= 4:
                    reader, count = read_at[m - 4]
                    pe.wait_ge(read_act if reader == "A" else read_dve, count)
                return psum[4 + m % 4]

            def end_job(ins):
                job[0] += 1
                ins.then_inc(job_done, 1)

            def arrive(kind, n):
                c = chunk_no[kind, n]
                pe.wait_ge(ring_landed[c % RING], landed[c])
                return chunk_of(kind, n)

            pe.wait_ge(consts_ready, 1)
            pe.wait_ge(vecs_landed, 16 * 13)
            for kind, n, _ in plan:
                if kind == "lru":
                    h, d = n // 2, n % 2
                    w = arrive("lru", n)[:, 0:1024].rearrange("p (q k n) -> p q k n", q=2, k=2)
                    if d == 0:
                        pe.wait_ge(conv_done, 2 * h + 2)
                    if n:
                        pe.wait_ge(gates_read, n)
                    for q in range(2):
                        for j in range(2):
                            for k in range(2):
                                last = mm(psum[2 * q + j][:, :], w[:, q, k, j * P:(j + 1) * P],
                                          xc[:, 2 * h + k, :], start=(k == 0), stop=(k == 1))
                    last.then_inc(gates_done, 1)
                    continue
                if kind == "xt" and n == 0:
                    pe.wait_ge(tok_scaled, 4)
                if kind == "xr" and n == 0:
                    pe.wait_ge(read_act, read_at[number["xt", KT - 2]][1])
                    pe.wait_ge(read_dve, read_at[number["xt", KT - 1]][1])
                if kind == "mod" and n == 0:
                    pe.wait_ge(silu_ready, 1)
                b = start_job()
                if kind == "vec":
                    nc.tensor.transpose(b[:, 0:P], vstage[:, 0:P], ident[:, :])
                    end_job(nc.tensor.transpose(b[:, P:P + 64], vstage[0:64, P:2 * P], ident[0:64, 0:64]))
                elif kind == "b1":
                    pe.wait_ge(late_landed, 16 * 3)
                    for q in range(4):
                        last = nc.tensor.transpose(b[:, q * P:(q + 1) * P], b1stage[:, q, :], ident[:, :])
                    end_job(last)
                elif kind == "mod":
                    w = arrive("mod", n).rearrange("p (k n) -> p k n", k=KT)
                    for k in range(KT):
                        last = mm(b[0:2, 0:CHUNK], sT[:, 2 * k:2 * k + 2], w[:, k, :], start=(k == 0), stop=(k == KT - 1))
                    end_job(last)
                elif kind == "mt":
                    pe.wait_ge(read_dve, read_at[number["mod", 7]][1])
                    for j in range(16):
                        last = nc.tensor.transpose(b[:, 2 * j:2 * j + 2], modrow[:, j * P:(j + 1) * P], ident[0:2, 0:2])
                    end_job(last)
                elif kind == "xt":
                    for t in range(4):
                        last = nc.tensor.transpose(b[:, t * P:(t + 1) * P], xin[:, t, n * P:(n + 1) * P], ident[:, :])
                    end_job(last)
                elif kind == "xr":
                    w = arrive("xr", n - n % 2).rearrange("p (k n) -> p k n", k=KT)
                    j = n % 2
                    for k in range(KT):
                        last = mm(b[:, :], w[:, k, j * P:(j + 1) * P], uT[:, k, :], start=(k == 0), stop=(k == KT - 1))
                    end_job(last)
                elif kind in ("xp", "gg", "mr", "mp", "rp", "pp"):
                    if kind == "rp" and n == 0:
                        pe.wait_ge(yrnn_ready, 1)
                    if kind == "pp" and n == 0:
                        pe.wait_ge(read_act, read_at[number["pw", 3]][1])
                    w = arrive(kind, n).rearrange("p (k n) -> p k n", k=KT)
                    src = {"rp": gT, "pp": ypT}.get(kind, uT[:, :, CTX:TOK])
                    for j in range(2):
                        for k in range(KT):
                            last = mm(b[:, j * SEQ:(j + 1) * SEQ], w[:, k, j * P:(j + 1) * P], src[:, k, :],
                                      start=(k == 0), stop=(k == KT - 1))
                    end_job(last)
                elif kind == "pw":
                    if n == 0:
                        pe.wait_ge(pool_ready, 4)
                        arrive("pw", 0)
                    w = chunk_of("pw", 0).rearrange("p (g k n) -> p g k n", g=4, k=2)
                    for j in range(2):
                        for k in range(2):
                            last = mm(b[:, j * SEQ:(j + 1) * SEQ], w[:, n, k, j * P:(j + 1) * P],
                                      xpp[:, n, k * ROWS:(k + 1) * ROWS, PAD:PAD + ROW], start=(k == 0), stop=(k == 1))
                    end_job(last)
                elif kind == "rs":
                    pe.wait_ge(sums_ready, 2 * n + 2)
                    for q in range(2):
                        last = mm(b[:, q * CHUNK:(q + 1) * CHUNK], ones[:, :], colsum(2 * n + q), start=True, stop=True)
                    end_job(last)
                elif kind == "wo":
                    w = arrive("wo", n).rearrange("p (k n) -> p k n", k=KT)
                    if n == 0:
                        pe.wait_ge(merged_ready, 4)
                    for t in range(TT):
                        for k in range(KT):
                            last = mm(b[:, t * CHUNK:(t + 1) * CHUNK], mgT[:, k, t * P:(t + 1) * P], w[:, k, :],
                                      start=(k == 0), stop=(k == KT - 1))
                    end_job(last)
                elif kind == "vt":
                    for t in range(TT):
                        if n == 0:
                            pe.wait_ge(v_ready, t + 1)
                        for kk in range(2):
                            k = 2 * n + kk
                            last = nc.tensor.transpose(b[:, kk * SEQ + t * P:kk * SEQ + (t + 1) * P],
                                                       vtok[:, t, k * P:(k + 1) * P], ident[:, :])
                    end_job(last)
                elif kind == "lg":
                    pe.wait_ge(read_act, read_at[number["vt", 2]][1])
                    pe.wait_ge(read_dve, read_at[number["vt", 3]][1])
                    for t in range(TT):
                        for k in range(KT):
                            last = mm(b[:, t * E:(t + 1) * E], vT[:, k, t * P:(t + 1) * P], rw[:, k * E:(k + 1) * E],
                                      start=(k == 0), stop=(k == KT - 1))
                    end_job(last)
                elif kind == "rk":
                    pe.wait_ge(mask_ready, 1)
                    mm(b[:, 0:E], upper[:, :], mask[:, 0, :], start=True, stop=True)
                    mm(b[:, E:2 * E], upper[:, :], mask[:, 1, :], start=True, stop=False)
                    mm(b[:, E:2 * E], ones[:, :], mask[:, 0, :], start=False, stop=True)
                    mm(b[:, 2 * E:3 * E], ones[:, :], mask[:, 0, :], start=True, stop=False)
                    end_job(mm(b[:, 2 * E:3 * E], ones[:, :], mask[:, 1, :], start=False, stop=True))
                elif kind == "ct":
                    pe.wait_ge(comb_ready, 1)
                    for t in range(TT):
                        last = nc.tensor.transpose(b[0:E, t * P:(t + 1) * P], comb_v[:, t, :], ident[:, :])
                    end_job(last)

            def bank_read(b):
                reader, count = read_at[max(n for n in range(JOBS) if 4 + n % 4 == b)]
                pe.wait_ge(read_act if reader == "A" else read_dve, count)

            def gather():
                for k in range(KT):
                    for t in range(TT):
                        last = mm(psum[7][:, k * SLOTS:(k + 1) * SLOTS], vtok[:, t, k * P:(k + 1) * P], sel[:, t, :],
                                  start=(t == 0), stop=(t == TT - 1))
                last.then_inc(gather_done, 1)

            def chunk(i, c, stat):
                if c < CPI:
                    b, q = block_of(c)
                    pe.wait_ge(hi_done, i * CPI + (c + 1))
                    lo_wait(pe, i, c)
                    for k in range(4):
                        lhs = stat[:, 4 * q + k].rearrange("p q c -> p (q c)")
                        for n, w in enumerate((whi[c % HIS], wlo[c])):
                            last = mm(psum[4 + b % 2][:, :], lhs, w[:, k, :],
                                      start=(q == 0 and k == 0 and n == 0), stop=(q == 1 and k == 3 and n == 1))
                    last.then_inc(w_used, 1)

            def fold(i, b):
                pe.wait_ge(z_ready, i * 4 + (b + 1))
                o = (b % 2) * 256
                for f in range(4):
                    last = mm(psum[6][:, o + f * SLOTS:o + (f + 1) * SLOTS], zS[b % 2][:, f * P:(f + 1) * P],
                              folder[:, :], start=True, stop=True)
                last.then_inc(fold_done, 1)

            def spread():
                for t in range(TT):
                    last = nc.tensor.transpose(psum[7][:, t * P:(t + 1) * P], selw[:, t, :], ident[:, :])
                last.then_inc(gt_done, 1)

            def scatter(halves=(0, 1)):
                for half in halves:
                    for t in range(TT):
                        last = mm(psum[2 * t + half][:, :], gt[:, t * P:(t + 1) * P], yS[:, half * 512:(half + 1) * 512],
                                  start=False, stop=False, skip_group_check=True)
                    last.then_inc(scatter_done, 1)

            def bias_rows():
                pe.wait_ge(read_dve, read_at[number["ct", 0]][1])
                pe.wait_ge(late_landed, 16 * 4)
                pe.wait_ge(gates_read, 2 * HEADS)
                for t in range(TT):
                    for half in range(2):
                        mm(psum[2 * t + half][:, :], combT[:, t * P:(t + 1) * P], b2s[:, half * 512:(half + 1) * 512],
                           start=True, stop=False, skip_group_check=True)

            def item(i, first=False, last=False):
                pe.wait_ge(xhi_ready, i + 1)
                pe.wait_ge(xlo_ready, i + 1)
                if first:
                    bank_read(4)
                    bank_read(5)
                else:
                    pe.wait_ge(y_ready, i * 2 - 1)
                chunk(i, 0, xhl)
                chunk(i, 1, xhl)
                if not first:
                    pe.wait_ge(y_ready, i * 2)
                chunk(i, 2, xhl)
                chunk(i, 3, xhl)
                if first:
                    pe.wait_ge(items_ready, 1)
                fold(i, 0)
                if first:
                    bias_rows()
                else:
                    scatter()
                pe.wait_ge(selw_ready, i + 1)
                spread()
                chunk(i, 4, xhl)
                chunk(i, 5, xhl)
                pe.wait_ge(glu_ready, i * 2 + 1)
                fold(i, 1)
                chunk(i, 6, xhl)
                chunk(i, 7, xhl)
                pe.wait_ge(act_ready, i * 2 + 1)
                fold(i, 2)
                pe.wait_ge(ahi_ready, i * 2 + 1)
                pe.wait_ge(alo_ready, i * 2 + 1)
                chunk(i, 8, ahl)
                pe.wait_ge(glu_ready, i * 2 + 2)
                fold(i, 3)
                chunk(i, 9, ahl)
                if not last:
                    pe.wait_ge(sel_ready, i + 2)
                    pe.wait_ge(gt_ready, i + 1)
                    gather()
                pe.wait_ge(ahi_ready, i * 2 + 2)
                pe.wait_ge(alo_ready, i * 2 + 2)
                chunk(i, 10, ahl)
                chunk(i, 11, ahl)

            pe.wait_ge(sel_ready, 1)
            bank_read(7)
            gather()
            pe.wait_ge(table_ready, 1)
            bank_read(6)
            for q in range(2):
                last = mm(psum[6][0:1, q * MORE:(q + 1) * MORE], tabf[:, q:q + 1], ident[0:MORE, 0:MORE],
                          start=True, stop=True)
            last.then_inc(table_done, 1)
            item(0, first=True)
            last_item = pe.value_load(more[0:1, 0:1], min_val=0, max_val=MORE - 1) + (E - 1)
            with pe.Fori(1, last_item) as i:
                item(i)
            item(last_item, last=True)
            pe.wait_ge(gt_ready, last_item + 1)
            for half in range(2):
                pe.wait_ge(y_ready, last_item * 2 + (half + 1))
                scatter((half,))

        @block.scalar
        def _(act):
            a = nc.scalar
            load_vectors(act, (ROWS1 + ROWS2)[1::2])
            act.dma_start(b1stage, I["exp_b1"][0].rearrange("e (f q) -> (e f) q", q=P).rearrange(
                "(n r) q -> r n q", r=P)).then_inc(late_landed, 16)
            act.dma_start(rw[:, :].rearrange("p (k e) -> p k e", k=KT),
                          I["router_w"][0].rearrange("(k p) e -> p k e", p=P)).then_inc(late_landed, 16)
            act.dma_start(rb[:, :], I["router_b"].broadcast_to([P, E])).then_inc(late_landed, 16)
            chain = [0]

            def link(ins):
                chain[0] += 1
                ins.then_inc(act_chain, 1)
                act.wait_ge(act_chain, chain[0])

            def job_of(kind, n):
                act.wait_ge(job_done, number[kind, n] + 1)
                return bank_of(kind, n)

            act.wait_ge(read_dve, 1)
            a.activation(small[:, 0:16], vecT[:, 0:16], ACT.Tanh, scale=0.5).then_inc(silu_th, 1)
            act.wait_ge(lam_abs, 1)
            a.activation(lamw[:, 16:32], lamw[:, 0:16], ACT.Exp, scale=-1.0).then_inc(lam_exp, 1)
            act.wait_ge(tokens_landed, 32)
            for t in range(4):
                ins = a.activation(arena[:, 16384:16384 + D], xin[:, t, :], ACT.Square, accum_out=stat[:, t:t + 1])
                ins.then_inc(ssq_ready, 1)
                act.wait_ge(ssq_ready, t + 1)
            act.wait_ge(rstd_var, 1)
            a.activation(stat[:, 8:12], stat[:, 4:8], ACT.Sqrt).then_inc(rstd_root, 1)

            act.wait_ge(mod_ready, 1)
            for k in range(0, KT, 2):
                b = job_of("xt", k)
                for s in range(2):
                    m = 1 - s
                    ins = a.activation(uT[:, k, s * CTX:(s + 1) * CTX], b[:, s * CTX:(s + 1) * CTX], ACT.Identity,
                                       bias=modT[:, 2 * k + m:2 * k + m + 1], scale=amod[:, 2 * k + m:2 * k + m + 1])
                ins.then_inc(read_act, 1)
            act.wait_ge(pads_ready, 1)
            for j in range(KT):
                b = job_of("xr", j)
                a.activation(xrp[:, j, :, 2:2 + CTX], b[:, :].rearrange("p (s t) -> p s t", s=2),
                             ACT.Copy).then_inc(read_act, 1)
            act.wait_ge(lru_consts, 1)
            for s in range(2 * HEADS):
                h, d = s // 2, s % 2
                act.wait_ge(gates_done, s + 1)
                if s:
                    act.wait_ge(lru_done, s)
                for j in range(2):
                    c = d * KT + 2 * h + j
                    a.activation(thr[:, j, :], psum[j][:, :], ACT.Tanh, bias=lamw[:, 64 + c:65 + c], scale=0.5)
                    ins = a.activation(thi[:, j, :], psum[2 + j][:, :], ACT.Tanh, bias=lamw[:, 80 + c:81 + c], scale=0.5)
                ins.then_inc(gates_read, 1)
                act.wait_ge(gates_read, s + 1)
                for j in range(2):
                    c = d * KT + 2 * h + j
                    a.activation(tnh[:, j, :], thr[:, j, :], ACT.Tanh, bias=lamw[:, 96 + c:97 + c],
                                 scale=lamw[:, 96 + c:97 + c])
                    ins = a.activation(dec[:, j, :], thr[:, j, :], ACT.Exp, bias=lamw[:, 112 + c:113 + c],
                                       scale=lamw[:, 112 + c:113 + c])
                link(ins)
                a.activation(rt, tnh, ACT.Sqrt).then_inc(coef_ready, 1)
                if s < 4:
                    b = job_of("xp", s)
                    ins = a.activation(xpp[:, s, :, PAD:PAD + ROW], b[:, :].rearrange("p (r q) -> p r q", q=ROW), ACT.Copy)
                    ins.then_inc(read_act, 1)
                else:
                    b = job_of("gg", s - 4)
                    a.activation(gbuf[:, (s - 4) * 512:(s - 3) * 512], b[:, :], ACT.Copy).then_inc(read_act, 1)
            act.wait_ge(read_act, read_at[number["gg", 3]][1])
            a.activation(gbuf[:, :], gbuf[:, :], ACT.Gelu_apprx_tanh).then_inc(gelu_ready, 1)
            for kind, dst in (("mr", m1), ("mp", m2)):
                for c in range(4):
                    b = job_of(kind, c)
                    a.activation(dst[:, c * 512:(c + 1) * 512], b[:, :], ACT.Tanh, scale=0.5).then_inc(read_act, 1)
            for gi in range(4):
                b = job_of("pw", gi)
                for j in range(2):
                    c = COL["pool_scale"] + 2 * gi + j
                    ins = a.activation(ypT[:, 2 * gi + j, :], b[:, j * SEQ:(j + 1) * SEQ], ACT.Copy,
                                       scale=vecT[:, c:c + 1])
                ins.then_inc(read_act, 1)

            def make_hi(i, c):
                act.wait_ge(expert_landed[c], 16 * i + 16)
                if not (isinstance(i, int) and i * CPI + c < HIS):
                    act.wait_ge(w_used, i * CPI + (c + 1 - HIS))
                a.activation(flat(whi[c % HIS]), flat(raw[c]), ACT.Copy).then_inc(hi_done, 1)

            a.activation(stat[:, 16:18], ones[:, 0:2], ACT.Sqrt).then_inc(act_warm, 1)
            act.wait_ge(act_warm, 1)
            act.wait_ge(job_done, number["rp", 3] + 1)
            for c in range(4):
                b = job_of("wo", c)
                ins = a.activation(mlat[:, :, c * CHUNK:(c + 1) * CHUNK], b[:, :].rearrange("p (t n) -> p t n", t=TT),
                                   ACT.Copy, scale=0.5)
                ins.then_inc(read_act, 1)
                act.wait_ge(read_act, read_at[number["wo", c]][1])
                for t in range(TT):
                    a.activation(bufB[:, t * CHUNK:(t + 1) * CHUNK], mlat[:, t, c * CHUNK:(c + 1) * CHUNK], ACT.Square,
                                 accum_out=small[:, 64 + 4 * t + c:65 + 4 * t + c]).then_inc(ssq2_ready, 1)
                act.wait_ge(ssq2_ready, 2 * c + 2)
                if c == 2:
                    make_hi(0, 0)
            act.wait_ge(var2, 1)
            a.activation(stat[:, 16:18], stat[:, 14:16], ACT.Sqrt).then_inc(root2, 1)
            make_hi(0, 1)
            for t in range(TT):
                act.wait_ge(x1_ready, t + 1)
                a.activation(bufB[:, t * D:(t + 1) * D], x1[:, t, :], ACT.Square,
                             accum_out=stat[:, 20 + t:21 + t]).then_inc(ssq3_ready, 1)
            act.dma_start(b2s, I["exp_b2"][0]).then_inc(late_landed, 16)
            act.wait_ge(var3, 1)
            a.activation(stat[:, 24:26], stat[:, 22:24], ACT.Sqrt).then_inc(root3, 1)
            make_hi(0, 2)
            make_hi(0, 3)
            for n in (0, 2):
                b = job_of("vt", n)
                ins = a.activation(m2[:, n * 512:(n + 1) * 512], b[:, :], ACT.Copy)
                ins.then_inc(read_act, 1)
            act.wait_ge(neg_max, 1)
            for t in range(TT):
                a.activation(ew[:, t, :], mx[:, t, 0:TOPK], ACT.Exp, bias=stat[:, 28 + t:29 + t],
                             accum_out=stat[:, 30 + t:31 + t]).then_inc(exps_ready, 1)

            def take_tokens(n):
                act.wait_ge(gather_done, n)
                a.activation(xhl[:, :, 0, :], psum[7][:, :].rearrange("p (k c) -> p k c", k=KT),
                             ACT.Copy).then_inc(xhi_ready, 1)

            def take_block(i, c):
                b, _ = block_of(c)
                act.wait_ge(w_used, i * CPI + (c + 1))
                dst = zS[b % 2] if b < 4 else yS[:, (b - 4) * 512:(b - 3) * 512]
                a.activation(dst, psum[4 + b % 2][:, :], ACT.Copy).then_inc(z_ready if b < 4 else y_ready, 1)

            def sigmoid(i, p):
                act.wait_ge(glu_ready, i * 2 + (p + 1))
                a.activation(sg, glu, ACT.Sigmoid, scale=ALPHA).then_inc(sig_ready, 1)

            def act_hi(i, p):
                act.wait_ge(act_ready, i * 2 + (p + 1))
                a.activation(ahl[:, 4 * p:4 * p + 4, 0, :], actf.rearrange("p (f c) -> p f c", f=4),
                             ACT.Copy).then_inc(ahi_ready, 1)

            def item(i, last=False):
                def ahead(c):
                    n = c + AHEAD
                    if isinstance(i, int) and i * CPI + n < HIS:
                        return
                    if n < CPI:
                        make_hi(i, n)
                    elif not last:
                        make_hi(i + 1, n - CPI)

                ahead(0)
                ahead(1)
                take_block(i, 1)
                ahead(2)
                ahead(3)
                take_block(i, 3)
                ahead(4)
                sigmoid(i, 0)
                act.wait_ge(gt_done, i + 1)
                a.activation(gt, psum[7][:, 0:SEQ], ACT.Copy).then_inc(gt_ready, 1)
                ahead(5)
                take_block(i, 5)
                ahead(6)
                act_hi(i, 0)
                ahead(7)
                take_block(i, 7)
                ahead(8)
                sigmoid(i, 1)
                ahead(9)
                act_hi(i, 1)
                if not last:
                    take_tokens(i + 2)
                ahead(10)
                take_block(i, 10)
                ahead(11)
                take_block(i, 11)

            take_tokens(1)
            item(0)
            act.wait_ge(items_ready, 1)
            last_item = act.value_load(more[0:1, 0:1], min_val=0, max_val=MORE - 1) + (E - 1)
            with act.Fori(1, last_item) as i:
                item(i)
            item(last_item, last=True)
            a.activation(small[:, 40:42], ones[:, 0:2], ACT.Sqrt).then_inc(act_warm, 1)
            for half in range(2):
                act.wait_ge(scatter_done, last_item * 2 + (half + 1))
                for t in range(TT):
                    n = 2 * half + t
                    a.activation(gbuf[:, 0:512], psum[2 * t + half][:, :], ACT.Square,
                                 accum_out=small[:, 32 + n:33 + n]).then_inc(ssq4_ready, 1)
                    act.wait_ge(ssq4_ready, n + 1)
            act.wait_ge(act_warm, 2)
            act.wait_ge(var4, 1)
            a.activation(small[:, 40:42], small[:, 38:40], ACT.Sqrt).then_inc(root4, 1)

        @block.vector
        def _(dve):
            v = nc.vector
            chain = [0]

            def link(ins):
                chain[0] += 1
                ins.then_inc(dve_chain, 1)
                dve.wait_ge(dve_chain, chain[0])

            def job_of(kind, n):
                dve.wait_ge(job_done, number[kind, n] + 1)
                return bank_of(kind, n)

            def col(name, n=0, w=1):
                return vecT[:, COL[name] + n:COL[name] + n + w]

            dve.wait_ge(consts_ready, 2)
            pos = slotno[:, 0:ROW]
            for gi, w in enumerate((2, 4, 8, 16)):
                q = icnt[:, gi * ROW:(gi + 1) * ROW]
                t = m2[:, 0:ROW]
                link(v.tensor_scalar(t, pos, -1.0, float(ROW), ALU.mult, ALU.add))
                link(v.tensor_scalar(t, t, w / 2.0, None, ALU.min))
                link(v.tensor_scalar(q, pos, w / 2.0, None, ALU.min))
                link(v.tensor_tensor(q, q, t, ALU.add))
            v.reciprocal(icnt[:, :], icnt[:, :]).then_inc(consts_ready, 1)

            b = job_of("vec", 0)
            v.tensor_copy(vecT[:, :], b[:, 0:NVEC]).then_inc(read_dve, 1)
            dve.wait_ge(read_dve, 1)
            lam = col("lru_lambda", 0, 16)
            L = lambda n: lamw[:, 16 * n:16 * n + 16]
            link(v.tensor_scalar(L(2), lam, -1.0, None, ALU.mult))
            v.tensor_tensor(L(0), L(2), lam, ALU.max).then_inc(lam_abs, 1)
            dve.wait_ge(silu_th, 1)
            st = sT[:, :].rearrange("p (k s) -> p s k", s=2)
            cc = vecT[:, 0:16].rearrange("p (s k) -> p s k", s=2)
            th = small[:, 0:16].rearrange("p (s k) -> p s k", s=2)
            link(v.scalar_tensor_tensor(st, th, 1.0, cc, ALU.add, ALU.mult))
            v.tensor_scalar(sT[:, :], sT[:, :], 0.5, None, ALU.mult).then_inc(silu_ready, 1)
            dve.wait_ge(ssq_ready, 4)
            v.tensor_scalar(stat[:, 4:8], stat[:, 0:4], 1.0 / D, EPS, ALU.mult, ALU.add).then_inc(rstd_var, 1)
            dve.wait_ge(rstd_root, 1)
            link(v.reciprocal(stat[:, 8:12], stat[:, 8:12]))
            for t in range(4):
                v.tensor_scalar(xin[:, t, :], xin[:, t, :], stat[:, 8 + t:9 + t], None, ALU.mult).then_inc(tok_scaled, 1)
            dve.wait_ge(lam_exp, 1)
            link(v.tensor_scalar(L(3), L(1), 2.0, None, ALU.add))
            link(v.reciprocal(L(3), L(3)))
            link(v.tensor_tensor(L(1), L(1), L(3), ALU.mult))
            link(v.tensor_tensor(L(3), L(1), L(1), ALU.mult))
            link(v.tensor_scalar(L(0), L(3), 1.0 / 15, 1.0 / 13, ALU.mult, ALU.add))
            for n in (11, 9, 7, 5, 3, 1):
                link(v.tensor_tensor(L(0), L(0), L(3), ALU.mult))
                link(v.tensor_scalar(L(0), L(0), 1.0 / n, None, ALU.add))
            link(v.scalar_tensor_tensor(L(0), L(0), 2.0, L(1), ALU.mult, ALU.mult))
            link(v.tensor_scalar(L(2), L(2), 0.0, None, ALU.max))
            link(v.tensor_tensor(L(0), L(0), L(2), ALU.add))
            v.tensor_scalar(L(4), col("lru_ba", 0, 16), 0.5, None, ALU.mult)
            v.tensor_scalar(L(5), col("lru_bx", 0, 16), 0.5, None, ALU.mult)
            v.tensor_scalar(L(6), L(0), 2.0, None, ALU.mult)
            v.tensor_scalar(L(7), L(0), -4.0, None, ALU.mult).then_inc(lru_consts, 1)

            for c in range(8):
                b = job_of("mod", c)
                v.tensor_copy(modrow[:, c * CHUNK:(c + 1) * CHUNK], b[0:2, 0:CHUNK]).then_inc(read_dve, 1)
            b = job_of("mt", 0)
            bm = col("b_mod", 0, 16).rearrange("p (j s) -> p j s", s=1).broadcast_to([P, 16, 2])
            v.tensor_tensor(modT[:, :].rearrange("p (j s) -> p j s", s=2), b[:, 0:32].rearrange("p (j s) -> p j s", s=2),
                            bm, ALU.add).then_inc(read_dve, 1)
            dve.wait_ge(read_dve, read_at[number["mt", 0]][1])
            am = amod[:, :].rearrange("p (k s) -> p k s", s=2)
            gb = col("norm_pre_mix", 0, 8).rearrange("p (k s) -> p k s", s=1).broadcast_to([P, KT, 2])
            v.scalar_tensor_tensor(am, modT[:, 16:32].rearrange("p (k s) -> p k s", s=2), 1.0, gb,
                                   ALU.add, ALU.mult).then_inc(mod_ready, 1)
            b = job_of("b1", 0)
            v.tensor_copy(b1T[:, :], b[:, :]).then_inc(read_dve, 1)
            dve.wait_ge(mod_ready, 1)
            for k in range(1, KT, 2):
                b = job_of("xt", k)
                for s in range(2):
                    m = 1 - s
                    ins = v.tensor_scalar(uT[:, k, s * CTX:(s + 1) * CTX], b[:, s * CTX:(s + 1) * CTX],
                                          amod[:, 2 * k + m:2 * k + m + 1], modT[:, 2 * k + m:2 * k + m + 1],
                                          ALU.mult, ALU.add)
                ins.then_inc(read_dve, 1)
            dve.wait_ge(job_done, number["xt", KT - 1] + 1)
            for j in range(KT):
                dve.wait_ge(read_act, read_at[number["xr", j]][1])
                o = xc[:, j, :].rearrange("p (s t) -> p s t", s=2)
                link(v.tensor_scalar(o, xrp[:, j, :, 0:CTX], col("conv_w", j), col("conv_b", j), ALU.mult, ALU.add))
                for w in range(1, CONV):
                    ins = v.scalar_tensor_tensor(o, xrp[:, j, :, w:w + CTX], col("conv_w", w * KT + j), o,
                                                 ALU.mult, ALU.add)
                    if w < CONV - 1:
                        link(ins)
                ins.then_inc(conv_done, 1)
            for s in range(2 * HEADS):
                h, d = s // 2, s % 2
                dve.wait_ge(coef_ready, s + 1)
                xh = xc[:, 2 * h:2 * h + 2, :]
                v.scalar_tensor_tensor(amul, dec, 1.0, tnh, ALU.add, ALU.mult)
                v.scalar_tensor_tensor(rt, dec, 1.0, rt, ALU.add, ALU.mult)
                link(v.scalar_tensor_tensor(bb, thi, 1.0, xh, ALU.add, ALU.mult))
                v.tensor_scalar(amul, amul, -1.0, 1.0, ALU.mult, ALU.add)
                link(v.scalar_tensor_tensor(bb, bb, 0.5, rt, ALU.mult, ALU.mult))
                for j in range(2):
                    ca, cb = amul[:, j, 0:CTX], bb[:, j, 0:CTX]
                    if d:
                        ca, cb = ca[:, ::-1], cb[:, ::-1]
                    ins = v.tensor_tensor_scan(hs[:, j, 0:CTX], ca, cb, 0.0, ALU.mult, ALU.add)
                link(ins)
                for j in range(2):
                    ca, cb = amul[:, j, CTX:TOK], bb[:, j, CTX:TOK]
                    if d:
                        ca, cb = ca[:, ::-1], cb[:, ::-1]
                    o = hs[:, j, CTX:TOK] if d else hT[:, 2 * h + j, :]
                    ins = v.tensor_tensor_scan(o, ca, cb, hs[:, j, CTX - 1:CTX], ALU.mult, ALU.add)
                if d:
                    link(ins)
                    for j in range(2):
                        q = 2 * h + j
                        ins = v.tensor_tensor(hT[:, q, :], hT[:, q, :], hs[:, j, CTX:TOK][:, ::-1], ALU.add)
                ins.then_inc(lru_done, 1)
                dve.wait_ge(lru_done, s + 1)
            dve.wait_ge(gelu_ready, 1)
            v.scalar_tensor_tensor(gbuf[:, :], hbuf[:, :], 0.5 * 2, gbuf[:, :], ALU.mult, ALU.mult).then_inc(yrnn_ready, 1)
            for c in range(4):
                r = slice(c * 512, (c + 1) * 512)
                if c == 0:
                    dve.wait_ge(read_act, read_at[number["mp", 3]][1])
                b = job_of("rp", c)
                v.scalar_tensor_tensor(m1[:, r], m1[:, r], 1.0, b[:, :], ALU.add, ALU.mult).then_inc(read_dve, 1)
                b = job_of("pp", c)
                ins = v.scalar_tensor_tensor(m2[:, r], m2[:, r], 1.0, b[:, :], ALU.add, ALU.mult)
                ins.then_inc(read_dve, 1)
                dve.wait_ge(read_dve, read_at[number["pp", c]][1])
                v.tensor_tensor(bufB[:, 2048 + c * 512:2048 + (c + 1) * 512], m1[:, r], m2[:, r],
                                ALU.add).then_inc(merged_ready, 1)
            dve.wait_ge(brow_landed, 64)
            dve.wait_ge(nrow_landed, 48)
            for n in range(8):
                b = job_of("rs", n)
                r = rows[:, n // 2, (n % 2) * 512:(n % 2 + 1) * 512]
                v.tensor_tensor(r, r, b[:, :], ALU.add).then_inc(read_dve, 1)
            dve.wait_ge(read_dve, read_at[number["rs", 7]][1])
            v.tensor_tensor(rows[:, 0, :], rows[:, 0, :], nrow[:, 0, :], ALU.mult)
            v.scalar_tensor_tensor(rows[:, 1, :], rows[:, 1, :], 1.0, nrow[:, 1, :], ALU.add, ALU.mult)
            v.tensor_tensor(rows[:, 3, :], rows[:, 3, :], nrow[:, 2, :], ALU.mult).then_inc(rows_ready, 1)
            dve.wait_ge(rows_ready, 1)

            def make_lo(i, c):
                dve.wait_ge(hi_done, i * CPI + (c + 1))
                v.tensor_tensor(flat(wlo[c])[:, 0:DVE_COLS], flat(raw[c])[:, 0:DVE_COLS],
                                flat(whi[c % HIS])[:, 0:DVE_COLS].bitcast(F32), ALU.subtract).then_inc(lo_dve, 1)

            for c in range(4):
                dve.wait_ge(ssq2_ready, 2 * c + 2)
                r = slice(c * CHUNK, (c + 1) * CHUNK)
                gb = rows[:, 0:1, r].broadcast_to([P, TT, CHUNK])
                v.tensor_tensor(mlat[:, :, r], mlat[:, :, r], gb, ALU.mult)
            link(v.tensor_reduce(stat[:, 12:14], small[:, 64:72].rearrange("p (t c) -> p t c", t=TT), AX.X, ALU.add))
            v.tensor_scalar(stat[:, 14:16], stat[:, 12:14], 1.0 / D, EPS, ALU.mult, ALU.add).then_inc(var2, 1)
            dve.wait_ge(root2, 1)
            link(v.reciprocal(stat[:, 18:20], stat[:, 16:18]))
            dve.wait_ge(xres_landed, 16)
            for t in range(TT):
                v.scalar_tensor_tensor(x1[:, t, :], mlat[:, t, :], stat[:, 18 + t:19 + t], x1[:, t, :],
                                       ALU.mult, ALU.add).then_inc(x1_ready, 1)
                dve.wait_ge(x1_ready, t + 1)
                v.tensor_tensor(vtok[:, t, :], x1[:, t, :], rows[:, 1, :], ALU.mult)
            dve.wait_ge(ssq3_ready, TT)
            v.tensor_scalar(stat[:, 22:24], stat[:, 20:22], 1.0 / D, EPS, ALU.mult, ALU.add).then_inc(var3, 1)
            dve.wait_ge(root3, 1)
            link(v.reciprocal(stat[:, 26:28], stat[:, 24:26]))
            for t in range(TT):
                v.scalar_tensor_tensor(vtok[:, t, :], vtok[:, t, :], stat[:, 26 + t:27 + t], rows[:, 2, :],
                                       ALU.mult, ALU.add).then_inc(v_ready, 1)
            for n in (1, 3):
                b = job_of("vt", n)
                ins = v.tensor_copy(m2[:, n * 512:(n + 1) * 512], b[:, :])
                ins.then_inc(read_dve, 1)
            b = job_of("lg", 0)
            rbb = rb[:, :].rearrange("p (t e) -> p t e", t=1).broadcast_to([P, TT, E])
            ins = v.tensor_tensor(lg, b[:, 0:64].rearrange("p (t e) -> p t e", t=TT), rbb, ALU.add)
            ins.then_inc(read_dve, 1)
            dve.wait_ge(read_dve, read_at[number["lg", 0]][1])
            for t in range(TT):
                ins = v.max(mx[:, t, :], lg[:, t, :])
            link(ins)
            v.tensor_scalar(stat[:, 28:30], mx[:, :, 0], -1.0, None, ALU.mult).then_inc(neg_max, 1)
            for t in range(TT):
                ins = v.max_index(ixu[:, 8 * t:8 * t + 8], mx[:, t, :], lg[:, t, :])
            link(ins)
            link(v.tensor_copy(ixf, ixu[:, :].rearrange("p (t k) -> p t k", t=TT)))
            ib = ecol[:, 0:E].rearrange("p (k e) -> p k e", k=1).broadcast_to([P, TOPK, E])
            for t in range(TT):
                xb = ixf[:, t, 0:TOPK].rearrange("p (k e) -> p k e", e=1).broadcast_to([P, TOPK, E])
                ins = v.tensor_tensor(oh[:, t], ib, xb, ALU.is_equal)
            link(ins)
            v.tensor_reduce(mask, oh.rearrange("p t k e -> p t e k"), AX.X, ALU.add).then_inc(mask_ready, 1)
            dve.wait_ge(exps_ready, TT)
            link(v.reciprocal(small[:, 48:50], stat[:, 30:32]))
            for t in range(TT):
                ins = v.tensor_scalar(ew[:, t, :], ew[:, t, :], small[:, 48 + t:49 + t], None, ALU.mult)
            link(ins)
            for t in range(TT):
                wb = ew[:, t, :].rearrange("p (k e) -> p k e", e=1).broadcast_to([P, TOPK, E])
                ins = v.tensor_tensor(ohw[:, t], oh[:, t], wb, ALU.mult)
            link(ins)
            v.tensor_reduce(comb_v, ohw.rearrange("p t k e -> p t e k"), AX.X, ALU.add).then_inc(comb_ready, 1)
            b = job_of("rk", 0)
            dve.wait_ge(mask_ready, 1)
            link(v.scalar_tensor_tensor(rank[:, :], b[:, 0:64], 1.0, mask.rearrange("p t e -> p (t e)"), ALU.add, ALU.mult))
            link(v.tensor_scalar(rank[:, :], rank[:, :], -1.0, None, ALU.add))
            v.tensor_copy(cnt, b[0:MORE, 64:96]).then_inc(read_dve, 1)
            dve.wait_ge(comb_ready, 1)

            def one_hot(e, r):
                for t in range(TT):
                    ins = v.tensor_scalar(sel[:, t, :], slotno[:, ds(r * 128, SLOTS)], rank[:, ds(e + t * E, 1)], None,
                                          ALU.is_equal)
                ins.then_inc(sel_ready, 1)

            def weighted(e, r):
                for t in range(TT):
                    ins = v.tensor_scalar(selw[:, t, :], slotno[:, ds(r * 128, 128)], rank[:, ds(e + t * E, 1)],
                                          comb[:, ds(e + t * E, 1)], ALU.is_equal, ALU.mult)
                ins.then_inc(selw_ready, 1)

            one_hot(0, 0)
            weighted(0, 0)

            def take_tokens(n):
                dve.wait_ge(xhi_ready, n)
                v.tensor_tensor(xhl[:, :, 1, :], psum[7][:, :].rearrange("p (k c) -> p k c", k=KT),
                                xhl[:, :, 0, :].bitcast(F32), ALU.subtract).then_inc(xlo_ready, 1)

            dve.wait_ge(read_dve, read_at[number["rk", 0]][1])
            for r in range(3):
                ins = v.tensor_scalar(ovr[:, r, :], cnt, float(SLOTS * (r + 1)), None, ALU.is_gt)
            link(ins)
            link(v.tensor_reduce(ovs, ovr.rearrange("p r e -> p e r"), AX.X, ALU.add))
            link(v.tensor_tensor_scan(inc, ones[0:MORE, 0:E], ovs, 0.0, ALU.mult, ALU.add))
            v.tensor_copy(more[0:1, :], inc[0:1, E - 1:E])
            link(v.tensor_tensor(exc, inc, ovs, ALU.subtract))
            for r in range(3):
                ins = v.scalar_tensor_tensor(posr[:, r, :], exc, float(r + 1), ovr[:, r, :], ALU.add, ALU.mult)
            link(ins)
            for q, vals in enumerate((ecol, rcol)):
                ins = v.scalar_tensor_tensor(look[:, q, :], posr.rearrange("p r e -> p (r e)"), jcol[0:MORE, 0:1],
                                             vals[0:MORE, :], ALU.is_equal, ALU.mult)
            link(ins)
            v.tensor_reduce(tabf, look, AX.X, ALU.add).then_inc(table_ready, 1)
            b = job_of("ct", 0)
            v.tensor_copy(combT, b[0:E, 0:SEQ]).then_inc(read_dve, 1)
            for c in range(HIS):
                make_lo(0, c)
            v.tensor_copy(tabE[:, 0:E], ecol[0:1, 0:E])
            v.memset(tabR[:, 0:E], 0)
            take_tokens(1)
            dve.wait_ge(table_done, 1)
            v.tensor_copy(tabE[:, E:ITEMS], psum[6][0:1, 0:MORE])
            v.tensor_copy(tabR[:, E:ITEMS], psum[6][0:1, MORE:2 * MORE]).then_inc(items_ready, 1)
            dve.wait_ge(items_ready, 1)
            last_item = dve.value_load(more[0:1, 0:1], min_val=0, max_val=MORE - 1) + (E - 1)

            base = chain[0]
            CH = 6

            def item(i, last=False):
                def step(ins, n):
                    ins.then_inc(dve_chain, 1)
                    dve.wait_ge(dve_chain, i * CH + (base + n))

                def ahead(c):
                    n = c + AHEAD
                    if isinstance(i, int) and i * CPI + n < HIS:
                        return
                    if n < CPI:
                        make_lo(i, n)
                    elif not last:
                        make_lo(i + 1, n - CPI)

                def biased(p, half, dst):
                    dve.wait_ge(fold_done, i * 4 + (2 * p + half + 1))
                    bias = b1T[:, ds(e0 * 16 + (8 * half + 4 * p), 4)].rearrange("p (f c) -> p f c", c=1).broadcast_to(
                        [P, 4, SLOTS])
                    step(v.tensor_tensor(dst.rearrange("p (f c) -> p f c", f=4),
                                         psum[6][:, half * 256:half * 256 + 256].rearrange("p (f c) -> p f c", f=4),
                                         bias, ALU.add), 3 * p + half + 1)

                def gate(p):
                    biased(p, 0, glu)
                    v.tensor_scalar(glu, glu, LIMIT, None, ALU.min).then_inc(glu_ready, 1)

                def linear(p):
                    dve.wait_ge(glu_ready, i * 2 + (p + 1))
                    biased(p, 1, lin)
                    dve.wait_ge(sig_ready, i * 2 + (p + 1))
                    v.tensor_scalar(lin, lin, LIMIT, -LIMIT, ALU.min, ALU.max)
                    step(v.tensor_tensor(sg, glu, sg, ALU.mult), 3 * p + 3)
                    v.scalar_tensor_tensor(actf, lin, 1.0, sg, ALU.add, ALU.mult).then_inc(act_ready, 1)

                def act_lo(p):
                    dve.wait_ge(ahi_ready, i * 2 + (p + 1))
                    v.tensor_tensor(ahl[:, 4 * p:4 * p + 4, 1, :], actf.rearrange("p (f c) -> p f c", f=4),
                                    ahl[:, 4 * p:4 * p + 4, 0, :].bitcast(F32), ALU.subtract).then_inc(alo_ready, 1)

                e0 = dve.value_load(tabE[0:1, ds(i, 1)], min_val=0, max_val=E - 1)
                if not last:
                    e1 = dve.value_load(tabE[0:1, ds(i + 1, 1)], min_val=0, max_val=E - 1)
                    r1 = dve.value_load(tabR[0:1, ds(i + 1, 1)], min_val=0, max_val=3)
                ahead(0)
                if not last:
                    one_hot(e1, r1)
                ahead(1)
                ahead(2)
                ahead(3)
                ahead(4)
                gate(0)
                ahead(5)
                linear(0)
                ahead(6)
                act_lo(0)
                if not last:
                    dve.wait_ge(gt_done, i + 1)
                    weighted(e1, r1)
                ahead(7)
                gate(1)
                ahead(8)
                linear(1)
                ahead(9)
                act_lo(1)
                if not last:
                    take_tokens(i + 2)
                ahead(10)
                ahead(11)

            item(0)
            with dve.Fori(1, last_item) as i:
                item(i)
            item(last_item, last=True)
            fs = small[:, 32:36].rearrange("p (h t) -> p h t", t=TT)
            tail = [0]

            def then(ins):
                tail[0] += 1
                ins.then_inc(tail_chain, 1)
                dve.wait_ge(tail_chain, tail[0])

            for half in range(2):
                r = slice(half * 512, (half + 1) * 512)
                for t in range(TT):
                    dve.wait_ge(ssq4_ready, 2 * half + t + 1)
                    ins = v.tensor_tensor(mout[:, t, r], psum[2 * t + half][:, :], rows[:, 3, r], ALU.mult)
            then(ins)
            then(v.tensor_tensor(small[:, 36:38], fs[:, 0, :], fs[:, 1, :], ALU.add))
            v.tensor_scalar(small[:, 38:40], small[:, 36:38], 1.0 / D, EPS, ALU.mult, ALU.add).then_inc(var4, 1)
            dve.wait_ge(root4, 1)
            then(v.reciprocal(small[:, 42:44], small[:, 40:42]))
            for t in range(TT):
                v.scalar_tensor_tensor(x1[:, t, :], mout[:, t, :], small[:, 42 + t:43 + t], x1[:, t, :],
                                       ALU.mult, ALU.add).then_inc(out_ready, 1)


_INS = ["x", "c", "ctx", "c_ctx", "w_mod", "b_mod", "norm_pre_mix", "norm_post_mix", "norm_pre_ffn",
        "norm_post_ffn", "w_in", "conv_w", "conv_b", "lru_wa", "lru_ba", "lru_wx", "lru_bx", "lru_lambda",
        "pool_w", "pool_scale", "w_rnn_proj", "w_pool_proj", "w_out", "router_w", "router_b",
        "exp_w1", "exp_b1", "exp_w2", "exp_b2"]


def kernel(**inputs):
    import concourse.bacc as bacc
    from concourse.bass_utils import run_bass_kernel_spmd

    nc = bacc.Bacc("TRN2", target_bir_lowering=False, num_devices=1)
    arrays, aps = {}, {}
    for name in _INS:
        a = np.ascontiguousarray(inputs[name])
        arrays[f"in_{name}"] = a
        aps[name] = nc.dram_tensor(f"in_{name}", a.shape, mybir.dt.from_np(a.dtype), kind="ExternalInput").ap()
    out = nc.dram_tensor("out", (1, SEQ, D), F32, kind="ExternalOutput").ap()
    build(nc, aps, out)
    r = run_bass_kernel_spmd(nc, [arrays], core_ids=[0])
    return r.results[0]["out"]
```
